# Optimizing a Trainium2 kernel written in Bass

```python
import jax, jax.numpy as jnp
from jax import lax
import numpy as np
import math

D_MODEL = 1024
BATCH = 1
SEQ = 512
DEPTH = 1

HEAD_DIM = 64
N_FOX_HEADS = 8
N_SB_HEADS = 8
FOX_WIDTH = N_FOX_HEADS * HEAD_DIM
SB_WIDTH = N_SB_HEADS * HEAD_DIM
MIX_WIDTH = FOX_WIDTH + SB_WIDTH
IN_COLS = 3 * FOX_WIDTH + 3 * SB_WIDTH + N_FOX_HEADS
Q_BLOCK = 128
N_MEM = 256
N_MEM_HEADS = 4
MEM_HEAD_DIM = D_MODEL // N_MEM_HEADS
D_FF = ((8 * D_MODEL // 3 + 255) // 256) * 256
CONV_WIDTH = 3
EPS = 1e-6


def _rmsnorm(x, g):
    xf = x.astype(jnp.float32)
    y = xf * lax.rsqrt(jnp.mean(xf * xf, axis=-1, keepdims=True) + EPS)
    return (y * g.astype(jnp.float32)).astype(x.dtype)

def _heads(t, n):
    b, s, w = t.shape
    return t.reshape(b, s, n, w // n).transpose(0, 2, 1, 3)

def _merge(t):
    b, n, s, d = t.shape
    return t.transpose(0, 2, 1, 3).reshape(b, s, n * d)

def _sweep(fn, q, *per_query):
    b, h, s, d = q.shape
    n = s // Q_BLOCK
    qb = q.reshape(b, h, n, Q_BLOCK, d).transpose(2, 0, 1, 3, 4)
    extras = [e.reshape(b, h, n, Q_BLOCK).transpose(2, 0, 1, 3) for e in per_query]
    out = lax.map(lambda a: fn(*a), (jnp.arange(n), qb, *extras))
    return out.transpose(1, 2, 0, 3, 4).reshape(b, h, s, d)

def _fox_attention(q, k, v, log_f):
    s_len = q.shape[2]
    scale = HEAD_DIM ** -0.5
    c = jnp.cumsum(log_f.astype(jnp.float32), axis=-1)
    kpos = jnp.arange(s_len)

    def block(i, qi, ci):
        qpos = i * Q_BLOCK + jnp.arange(Q_BLOCK)
        logits = jnp.einsum('bhqd,bhkd->bhqk', qi, k, preferred_element_type=jnp.float32) * scale
        logits = logits + ci[..., None] - c[:, :, None, :]
        logits = jnp.where(kpos[None, :] <= qpos[:, None], logits, -jnp.inf)
        p = jax.nn.softmax(logits, axis=-1)
        return jnp.einsum('bhqk,bhkd->bhqd', p.astype(v.dtype), v)

    return _sweep(block, q, c)

def _stick_breaking_attention(q, k, v):
    s_len = q.shape[2]
    scale = HEAD_DIM ** -0.5
    kpos = jnp.arange(s_len)

    def block(i, qi):
        qpos = i * Q_BLOCK + jnp.arange(Q_BLOCK)
        z = jnp.einsum('bhqd,bhkd->bhqk', qi, k, preferred_element_type=jnp.float32) * scale
        strict = kpos[None, :] < qpos[:, None]
        log_keep = jnp.where(strict, jax.nn.log_sigmoid(-z), 0.0)
        after = lax.cumsum(log_keep, axis=3, reverse=True) - log_keep
        a = jnp.where(strict, jnp.exp(jax.nn.log_sigmoid(z) + after), 0.0)
        return jnp.einsum('bhqk,bhkd->bhqd', a.astype(v.dtype), v)

    return _sweep(block, q)

def _memory_cross_attention(h, m, w_q, w_kv, w_o):
    q = _heads(jnp.einsum('bsd,dc->bsc', h, w_q), N_MEM_HEADS)
    kv = jnp.einsum('bmd,dc->bmc', m, w_kv)
    k, v = jnp.split(kv, 2, axis=-1)
    k, v = _heads(k, N_MEM_HEADS), _heads(v, N_MEM_HEADS)
    logits = jnp.einsum('bhqd,bhkd->bhqk', q, k, preferred_element_type=jnp.float32) * (MEM_HEAD_DIM ** -0.5)
    p = jax.nn.softmax(logits, axis=-1)
    o = jnp.einsum('bhqk,bhkd->bhqd', p.astype(v.dtype), v)
    return jnp.einsum('bsc,cd->bsd', _merge(o), w_o)

def _causal_dwconv(u, w, b):
    s_len = u.shape[1]
    up = jnp.pad(u, ((0, 0), (CONV_WIDTH - 1, 0), (0, 0)))
    y = b
    for i in range(CONV_WIDTH):
        y = y + up[:, i:i + s_len] * w[i]
    return y

def first_inputs(seed: int = 0) -> dict:
    key = jax.random.key(seed)
    ks = jax.random.split(key, 24)
    f32 = jnp.float32

    def nrm(k, shape, fan_in):
        return jax.random.normal(k, shape, f32) * (fan_in ** -0.5)

    def gain(k, shape):
        return 1.0 + 0.02 * jax.random.normal(k, shape, f32)

    return {
        "x": jax.random.normal(ks[0], (BATCH, SEQ, D_MODEL), f32),
        "mem": jax.random.normal(ks[1], (BATCH, N_MEM, D_MODEL), f32),
        "attn_norm_g": gain(ks[2], (DEPTH, D_MODEL)),
        "w_in": nrm(ks[3], (DEPTH, D_MODEL, IN_COLS), D_MODEL),
        "b_forget": jnp.linspace(1.0, 6.0, N_FOX_HEADS, dtype=f32)[None, :]
                    + 0.1 * jax.random.normal(ks[4], (DEPTH, N_FOX_HEADS), f32),
        "fox_out_g": gain(ks[5], (DEPTH, FOX_WIDTH)),
        "sb_out_g": gain(ks[6], (DEPTH, SB_WIDTH)),
        "w_out": nrm(ks[7], (DEPTH, MIX_WIDTH, D_MODEL), MIX_WIDTH),
        "xattn_norm_g": gain(ks[8], (DEPTH, D_MODEL)),
        "mem_norm_g": gain(ks[9], (DEPTH, D_MODEL)),
        "w_mq": nrm(ks[10], (DEPTH, D_MODEL, D_MODEL), D_MODEL),
        "w_mkv": nrm(ks[11], (DEPTH, D_MODEL, 2 * D_MODEL), D_MODEL),
        "w_mo": nrm(ks[12], (DEPTH, D_MODEL, D_MODEL), D_MODEL),
        "ffn_norm_g": gain(ks[13], (DEPTH, D_MODEL)),
        "w_up": nrm(ks[14], (DEPTH, D_MODEL, 2 * D_FF), D_MODEL),
        "conv_w": nrm(ks[15], (DEPTH, CONV_WIDTH, 2 * D_FF), CONV_WIDTH),
        "conv_b": 0.02 * jax.random.normal(ks[16], (DEPTH, 2 * D_FF), f32),
        "w_down": nrm(ks[17], (DEPTH, D_FF, D_MODEL), D_FF),
        "final_norm_g": gain(ks[18], (D_MODEL,)),
    }

def first_block(x, mem, attn_norm_g, w_in, b_forget, fox_out_g, sb_out_g, w_out,
              xattn_norm_g, mem_norm_g, w_mq, w_mkv, w_mo,
              ffn_norm_g, w_up, conv_w, conv_b, w_down, final_norm_g):
    split_at = np.cumsum([FOX_WIDTH, FOX_WIDTH, FOX_WIDTH, SB_WIDTH, SB_WIDTH, SB_WIDTH]).tolist()
    for l in range(DEPTH):
        h = _rmsnorm(x, attn_norm_g[l])
        proj = jnp.einsum('bsd,dc->bsc', h, w_in[l])
        fq, fk, fv, sq, sk, sv, f_logit = jnp.split(proj, split_at, axis=-1)
        log_f = jax.nn.log_sigmoid(f_logit.astype(jnp.float32) + b_forget[l].astype(jnp.float32))
        log_f = log_f.transpose(0, 2, 1)
        fox_o = _merge(_fox_attention(_heads(fq, N_FOX_HEADS), _heads(fk, N_FOX_HEADS),
                                      _heads(fv, N_FOX_HEADS), log_f))
        sb_o = _merge(_stick_breaking_attention(_heads(sq, N_SB_HEADS), _heads(sk, N_SB_HEADS),
                                                _heads(sv, N_SB_HEADS)))
        mixed = jnp.concatenate([_rmsnorm(fox_o, fox_out_g[l]), _rmsnorm(sb_o, sb_out_g[l])], axis=-1)
        x = x + jnp.einsum('bsc,cd->bsd', mixed, w_out[l])

        h = _rmsnorm(x, xattn_norm_g[l])
        m = _rmsnorm(mem, mem_norm_g[l])
        x = x + _memory_cross_attention(h, m, w_mq[l], w_mkv[l], w_mo[l])

        h = _rmsnorm(x, ffn_norm_g[l])
        u = jnp.einsum('bsd,df->bsf', h, w_up[l])
        u = _causal_dwconv(u, conv_w[l], conv_b[l])
        gate, val = jnp.split(u, 2, axis=-1)
        x = x + jnp.einsum('bsf,fd->bsd', jax.nn.silu(gate) * val, w_down[l])
    return _rmsnorm(x, final_norm_g)


DEPTH_2 = 2

CHUNK = 64
N_A = DEPTH_2 // 2
N_B = DEPTH_2 - N_A
GMLP_BLOCK = 128
GATE_DIM = 2 * D_MODEL
A_GROUPS = 8
A_GROUP_DIM = GATE_DIM // A_GROUPS
B_HEADS = 8
QK_NOPE = 128
QK_ROPE = 64
V_HEAD = 128
Q_LORA = 384
KV_LORA = 256
ROPE_THETA = 10000.0
D_FF_2 = 4 * D_MODEL


def rmsnorm(x, g):
    xf = x.astype(jnp.float32)
    y = xf * lax.rsqrt(jnp.mean(xf * xf, axis=-1, keepdims=True) + EPS)
    return (y * g.astype(jnp.float32)).astype(x.dtype)

def layernorm(x, g, b):
    xf = x.astype(jnp.float32)
    mu = jnp.mean(xf, axis=-1, keepdims=True)
    var = jnp.mean(jnp.square(xf - mu), axis=-1, keepdims=True)
    y = (xf - mu) * lax.rsqrt(var + EPS)
    return (y * g.astype(jnp.float32) + b.astype(jnp.float32)).astype(x.dtype)

def rope_angles(positions):
    inv_freq = ROPE_THETA ** (-jnp.arange(0, QK_ROPE, 2, dtype=jnp.float32) / QK_ROPE)
    return positions.astype(jnp.float32)[..., None] * inv_freq

def apply_rope(x, ang):
    xf = x.astype(jnp.float32)
    x1, x2 = jnp.split(xf, 2, axis=-1)
    c, s = jnp.cos(ang), jnp.sin(ang)
    return jnp.concatenate([x1 * c - x2 * s, x2 * c + x1 * s], axis=-1).astype(x.dtype)

def chunk_mask(q_idx, k_idx):
    return (k_idx[None, :] // CHUNK) <= (q_idx[:, None] // CHUNK)

def gmlp_mixer(hn, w_in, ln_g, ln_b, w_s, b_s, w_out):
    B, S, _ = hn.shape
    z = jax.nn.gelu(hn @ w_in, approximate=False)
    u, v = jnp.split(z, 2, axis=-1)
    v = layernorm(v, ln_g, ln_b)
    nb = S // GMLP_BLOCK
    vb = v.reshape(B, nb, GMLP_BLOCK, A_GROUPS, A_GROUP_DIM)
    idx = jnp.arange(GMLP_BLOCK)
    ws = jnp.where(chunk_mask(idx, idx)[None], w_s, jnp.zeros_like(w_s))
    sv = jnp.einsum('gij,bnjgc->bnigc', ws, vb) + b_s.T[None, None, :, :, None]
    return (u * sv.reshape(B, S, GATE_DIM)) @ w_out

def shared_latent_kv(h, positions, src_g, w_kv_a, kv_a_g, w_kv_b):
    B, S, _ = h.shape
    hn = rmsnorm(h, src_g)
    ckv = hn @ w_kv_a
    c_kv, k_pe = ckv[..., :KV_LORA], ckv[..., KV_LORA:]
    c_kv = rmsnorm(c_kv, kv_a_g)
    kv = (c_kv @ w_kv_b).reshape(B, S, B_HEADS, QK_NOPE + V_HEAD)
    k_nope, v = kv[..., :QK_NOPE], kv[..., QK_NOPE:]
    k_pe = apply_rope(k_pe, rope_angles(positions))
    return k_nope, k_pe, v

def chunk_causal_mla_attention(q_nope, q_pe, k_nope, k_pe, v):
    B, S, H, _ = q_nope.shape
    nb = S // Q_BLOCK
    qn = q_nope.reshape(B, nb, Q_BLOCK, H, QK_NOPE).transpose(1, 0, 2, 3, 4)
    qp = q_pe.reshape(B, nb, Q_BLOCK, H, QK_ROPE).transpose(1, 0, 2, 3, 4)
    k_idx = jnp.arange(S)
    scale = (QK_NOPE + QK_ROPE) ** -0.5

    def one_block(args):
        qn_b, qp_b, i = args
        s = (jnp.einsum('bqhd,bkhd->bhqk', qn_b, k_nope).astype(jnp.float32)
             + jnp.einsum('bqhd,bkd->bhqk', qp_b, k_pe).astype(jnp.float32)) * scale
        q_idx = i * Q_BLOCK + jnp.arange(Q_BLOCK)
        s = jnp.where(chunk_mask(q_idx, k_idx)[None, None], s, jnp.finfo(jnp.float32).min)
        p = jax.nn.softmax(s, axis=-1).astype(v.dtype)
        return jnp.einsum('bhqk,bkhd->bqhd', p, v)

    out = lax.map(one_block, (qn, qp, jnp.arange(nb)))
    return out.transpose(1, 0, 2, 3, 4).reshape(B, S, H, V_HEAD)

def mla_mixer(hn, kv, positions, w_q_a, q_g, w_q_b, w_o):
    B, S, _ = hn.shape
    k_nope, k_pe, v = kv
    cq = rmsnorm(hn @ w_q_a, q_g)
    q = (cq @ w_q_b).reshape(B, S, B_HEADS, QK_NOPE + QK_ROPE)
    q_nope = q[..., :QK_NOPE]
    q_pe = apply_rope(q[..., QK_NOPE:], rope_angles(positions)[:, :, None, :])
    o = chunk_causal_mla_attention(q_nope, q_pe, k_nope, k_pe, v)
    return o.reshape(B, S, B_HEADS * V_HEAD) @ w_o

def sq_relu_mlp(hn, w1, w2):
    return jnp.square(jax.nn.relu(hn @ w1)) @ w2

def second_inputs(seed: int = 0) -> dict:
    key = jax.random.key(seed)
    ks = jax.random.split(key, 24)

    def nrm(k, shape, fan_in, mult=1.0):
        return jax.random.normal(k, shape, jnp.float32) * (mult * fan_in ** -0.5)

    def gain(k, shape):
        return 1.0 + 0.05 * jax.random.normal(k, shape, jnp.float32)

    x = jax.random.normal(ks[0], (BATCH, SEQ, D_MODEL), jnp.float32)
    offset = jax.random.randint(ks[1], (BATCH, 1), 0, 4096, dtype=jnp.int32)
    positions = offset + jnp.arange(SEQ, dtype=jnp.int32)[None, :]
    return {
        "x": x,
        "positions": positions,
        "norm_mix_g": gain(ks[2], (DEPTH_2, D_MODEL)),
        "norm_mlp_g": gain(ks[3], (DEPTH_2, D_MODEL)),
        "a_w_in": nrm(ks[4], (N_A, D_MODEL, 2 * GATE_DIM), D_MODEL),
        "a_ln_v_g": gain(ks[5], (N_A, GATE_DIM)),
        "a_ln_v_b": 0.02 * jax.random.normal(ks[6], (N_A, GATE_DIM), jnp.float32),
        "a_w_s": nrm(ks[7], (N_A, A_GROUPS, GMLP_BLOCK, GMLP_BLOCK), GMLP_BLOCK, 0.5),
        "a_b_s": 1.0 + 0.1 * jax.random.normal(ks[8], (N_A, A_GROUPS, GMLP_BLOCK), jnp.float32),
        "a_w_out": nrm(ks[9], (N_A, GATE_DIM, D_MODEL), GATE_DIM),
        "b_w_q_a": nrm(ks[10], (N_B, D_MODEL, Q_LORA), D_MODEL),
        "b_q_norm_g": gain(ks[11], (N_B, Q_LORA)),
        "b_w_q_b": nrm(ks[12], (N_B, Q_LORA, B_HEADS * (QK_NOPE + QK_ROPE)), Q_LORA),
        "b_w_o": nrm(ks[13], (N_B, B_HEADS * V_HEAD, D_MODEL), B_HEADS * V_HEAD),
        "kv_src_norm_g": gain(ks[14], (D_MODEL,)),
        "kv_w_a": nrm(ks[15], (D_MODEL, KV_LORA + QK_ROPE), D_MODEL),
        "kv_a_norm_g": gain(ks[16], (KV_LORA,)),
        "kv_w_b": nrm(ks[17], (KV_LORA, B_HEADS * (QK_NOPE + V_HEAD)), KV_LORA),
        "mlp_w1": nrm(ks[18], (DEPTH_2, D_MODEL, D_FF_2), D_MODEL),
        "mlp_w2": nrm(ks[19], (DEPTH_2, D_FF_2, D_MODEL), D_FF_2, 0.5),
        "final_norm_g": gain(ks[20], (D_MODEL,)),
    }

def second_block(x, positions, norm_mix_g, norm_mlp_g, a_w_in, a_ln_v_g, a_ln_v_b, a_w_s,
              a_b_s, a_w_out, b_w_q_a, b_q_norm_g, b_w_q_b, b_w_o, kv_src_norm_g, kv_w_a,
              kv_a_norm_g, kv_w_b, mlp_w1, mlp_w2, final_norm_g):
    h = x
    kv = None
    for l in range(DEPTH_2):
        hn = rmsnorm(h, norm_mix_g[l])
        if l < N_A:
            h = h + gmlp_mixer(hn, a_w_in[l], a_ln_v_g[l], a_ln_v_b[l], a_w_s[l],
                               a_b_s[l], a_w_out[l])
        else:
            j = l - N_A
            h = h + mla_mixer(hn, kv, positions, b_w_q_a[j], b_q_norm_g[j], b_w_q_b[j], b_w_o[j])
        h = h + sq_relu_mlp(rmsnorm(h, norm_mlp_g[l]), mlp_w1[l], mlp_w2[l])
        if l == N_A - 1:
            kv = shared_latent_kv(h, positions, kv_src_norm_g, kv_w_a, kv_a_norm_g, kv_w_b)
    return rmsnorm(h, final_norm_g)


def setup_inputs(seed=0):
    out = dict(first_inputs(seed))
    for name, value in second_inputs(seed + 1).items():
        if name != "x":
            out[name + "_2"] = value
    return out


def reference(
    x, mem, attn_norm_g, w_in, b_forget, fox_out_g, sb_out_g, w_out, xattn_norm_g, mem_norm_g,
    w_mq, w_mkv, w_mo, ffn_norm_g, w_up, conv_w, conv_b, w_down, final_norm_g, positions_2,
    norm_mix_g_2, norm_mlp_g_2, a_w_in_2, a_ln_v_g_2, a_ln_v_b_2, a_w_s_2, a_b_s_2, a_w_out_2,
    b_w_q_a_2, b_q_norm_g_2, b_w_q_b_2, b_w_o_2, kv_src_norm_g_2, kv_w_a_2, kv_a_norm_g_2,
    kv_w_b_2, mlp_w1_2, mlp_w2_2, final_norm_g_2,
):
    x = first_block(
        x, mem, attn_norm_g, w_in, b_forget, fox_out_g, sb_out_g, w_out, xattn_norm_g,
        mem_norm_g, w_mq, w_mkv, w_mo, ffn_norm_g, w_up, conv_w, conv_b, w_down, final_norm_g,
    )
    return second_block(
        x, positions_2, norm_mix_g_2, norm_mlp_g_2, a_w_in_2, a_ln_v_g_2, a_ln_v_b_2, a_w_s_2,
        a_b_s_2, a_w_out_2, b_w_q_a_2, b_q_norm_g_2, b_w_q_b_2, b_w_o_2, kv_src_norm_g_2,
        kv_w_a_2, kv_a_norm_g_2, kv_w_b_2, mlp_w1_2, mlp_w2_2, final_norm_g_2,
    )


_drawn_inputs = setup_inputs


def setup_inputs(seed=0):
    import zlib

    import numpy as np

    out = dict(_drawn_inputs(seed))
    spreads = {}
    factors = {'fox_out_g': 4.748,
     'sb_out_g': 4.637,
     'xattn_norm_g': 8.0,
     'mem_norm_g': 8.0,
     'ffn_norm_g': 4.35,
     'conv_b': 4.477,
     'a_ln_v_g_2': 4.817,
     'a_ln_v_b_2': 8.0,
     'b_q_norm_g_2': 8.0,
     'kv_src_norm_g_2': 4.44,
     'kv_a_norm_g_2': 3.653}
    for name, (base, spread) in spreads.items():
        noise = np.random.default_rng([zlib.crc32(name.encode()), seed]).standard_normal(out[name].shape)
        drawn = base * np.exp(spread * noise) if base else spread * noise
        out[name] = __import__('jax').numpy.asarray(drawn.astype(out[name].dtype))
    for name, factor in factors.items():
        out[name] = (out[name] * factor).astype(out[name].dtype)
    return out
```

```python
from contextlib import ExitStack, contextmanager

import numpy as np

import concourse.bass as bass
from concourse import mybir

F32 = mybir.dt.float32
F32R = mybir.dt.float32r
I32 = mybir.dt.int32
ALU = mybir.AluOpType
ACT = mybir.ActivationFunctionType
AX = mybir.AxisListType

P = 128
S = 512
D = 1024
KT = D // P
TT = S // P
NMEM = 256
MT = NMEM // P
HEADS = 8
HD = 64
MEM_HEADS = 4
D_FF = 2816
GATE = 2048
D_FF_2 = 4096
Q_LORA, KV_LORA = 384, 256
NOPE, ROPE, VH = 128, 64, 128
MLA_HEADS = 8
EPS = 1e-6
MASKED = -3.0e38
CONSTANTS = 14
SLOT = 2048
COLS = 256
GRAN = 256

VECTORS = [
    [("attn_norm_g", 8), ("fox_out_g", 4), ("sb_out_g", 4), ("xattn_norm_g", 8), ("mem_norm_g", 8),
     ("ffn_norm_g", 8), ("conv_w0", 44), ("conv_w1", 44)],
    [("conv_w2", 44), ("conv_b", 44), ("final_norm_g", 8), ("mix0", 8), ("mix1", 8), ("mlp0", 8), ("mlp1", 8)],
    [("a_ln_v_g_2", 16), ("a_ln_v_b_2", 16), ("b_q_norm_g_2", 3), ("kv_src_norm_g_2", 8),
     ("kv_a_norm_g_2", 2), ("final_norm_g_2", 8)],
]
COLUMN = {}
_at = 0
for _group in VECTORS:
    for _name, _rows in _group:
        COLUMN[_name] = _at
        _at += _rows
NVEC = _at


class Count:

    def __init__(self):
        self.n, self.reg, self.per = 0, None, 0

    def at(self, value):
        return value if self.reg is None else self.reg * self.per + value


@contextmanager
def loop(engine, times, counts):
    start = [c.n for c, _ in counts]
    with engine.Fori(0, times) as i:
        for c, per in counts:
            c.reg, c.per = i, per
        yield i
    for (c, per), n in zip(counts, start):
        assert c.n - n == per, (c.n - n, per)
        c.n, c.reg = n + per * times, None


def weight_stream(w):
    def columns(name, first, n=COLS, tiles=2, stride=0):
        v = w[name].rearrange("(k p) n -> p k n", p=P)
        def parts(raw, i):
            return [(raw.rearrange("p (k n) -> p k n", n=COLS)[:, :, 0:n], v[:, :, bass.ds(i * stride + first, n)])]
        return SLOT, tiles, parts, max(n, P)

    def rows(name, granule, stride=0):
        v = w[name].rearrange("(k p) n -> p k n", p=P)
        def parts(raw, i):
            return [(raw.rearrange("p (k n) -> p k n", k=2), v[:, bass.ds(i * stride + 2 * granule, 2), :])]
        return SLOT, KT, parts, 0

    def k_rope(raw, i):
        v = w["kv_w_a_2"].rearrange("(k p) n -> p k n", p=P)
        d = raw.rearrange("p (k n) -> p k n", n=COLS)
        a, b = v[:, :, KV_LORA:KV_LORA + 32], v[:, :, KV_LORA + 32:KV_LORA + 64]
        return [(d[:, :, 0:32], a), (d[:, :, 32:64], b), (d[:, :, 64:96], b), (d[:, :, 96:128], a)]

    def q_heads(pair):
        v = w["b_w_q_b_2"].rearrange("(k p) n -> p k n", p=P)
        def parts(raw, i):
            d = raw[:, 0:3 * 512].rearrange("p (k n) -> p k n", n=512)
            out = []
            for j in range(2):
                at = (2 * pair + j) * (NOPE + ROPE)
                out += [(d[:, :, 256 * j:256 * j + 192], v[:, :, at:at + 192]),
                        (d[:, :, 256 * j + 192:256 * j + 224], v[:, :, at + 160:at + 192]),
                        (d[:, :, 256 * j + 224:256 * j + 256], v[:, :, at + 128:at + 160])]
            return out
        return 3 * 512, 4, parts, 0

    def kv_heads(c):
        v = w["kv_w_b_2"].rearrange("(k p) n -> p k n", p=P)
        return SLOT, 8, lambda raw, i: [(raw.rearrange("p (k n) -> p k n", k=2), v[:, :, 1024 * c:1024 * c + 1024])], 0

    def mlp(up, down):
        u = lambda g, s=0: columns(up, COLS * g, stride=s)
        d = lambda g, s=0: rows(down, g, stride=s)
        return [u(0), u(1), ("loop", 7, [d(0, 4), u(2, 512), d(1, 4), u(3, 512)]), d(14), d(15)]

    g = lambda n, s=0: columns("w_up", COLS * n, stride=s)
    v = lambda n, s=0: columns("w_up", D_FF + COLS * n, stride=s)
    d = lambda n, s=0: rows("w_down", n, stride=s)
    out = [("tiles", 2 * KT)]
    for base in (0, 3 * HEADS * HD):
        out += [columns("w_in", base + COLS * c) for c in range(4)]
        out += [columns("w_in", 6 * HEADS * HD, n=HEADS, tiles=1)] if base == 0 else []
        out += [columns("w_in", base + 1024 + COLS * c) for c in range(2)]
        out += ([columns("w_mkv", COLS * c) for c in range(4)] if base == 0 else
                [columns("w_mkv", COLS * c, tiles=1) for c in range(4, 8)])
    out += [rows("w_out", c) for c in range(4)]
    out += [columns("w_mq", COLS * c) for c in range(4)] + [rows("w_mo", c) for c in range(4)]
    out += [g(0), v(0), g(1), v(1), ("loop", 4, [d(0, 4), g(2, 512), v(2, 512), d(1, 4), g(3, 512), v(3, 512)]),
            d(8), g(10), v(10), d(9), d(10)]
    out += [columns("a_w_in_2", GATE + COLS * c) for c in range(8)]
    out += [("tiles", 4)] + [columns("a_w_in_2", COLS * c) for c in range(8)]
    out += [("tiles", 2)]
    for c in range(8):
        out += [("tiles", 2)] * (c < 7) + [rows("a_w_out_2", c)]
    out += mlp("w1_0", "w2_0")
    out += [columns("b_w_q_a_2", 0), columns("b_w_q_a_2", 256, n=128, tiles=1)]
    out += [columns("kv_w_a_2", 0), (SLOT, 1, k_rope, P)]
    out += [q_heads(p) for p in range(4)] + [kv_heads(c) for c in range(2)]
    out += [rows("b_w_o_2", c) for c in range(4)]
    out += mlp("w1_1", "w2_1")
    return out


def build(nc, w, out, stop=99):
    x_in, mem_in = w["x"], w["mem"]
    freq = nc.inline_tensor(np.tile((np.float32(10000.0) ** (-np.arange(0, ROPE, 2, dtype=np.float32)
                                    / np.float32(ROPE))).astype(np.float32), 4).reshape(P, 1), name="inv_freq")

    with ExitStack() as ctx:
        def sb(name, shape, dt=F32):
            return ctx.enter_context(nc.sbuf_tensor(name, shape, dt))

        def sem(name):
            return ctx.enter_context(nc.semaphore(name))

        raw = sb("raw", [P, 2, SLOT])
        w_hi = sb("w_hi", [P, 2, SLOT], F32R)
        w_lo = sb("w_lo", [P, 2, SLOT], F32R)
        x = sb("resid", [P, KT, S])
        h_hi = sb("h_hi", [P, KT, S], F32R)
        h_lo = sb("h_lo", [P, KT, S], F32R)
        g_hi = sb("g_hi", [P, 4, S], F32R)
        g_lo = sb("g_lo", [P, 4, S], F32R)
        vec = sb("vec", [P, NVEC])
        ident = sb("ident", [P, P])
        ones = sb("ones", [P, P])
        causal = sb("causal", [P, P])
        strict = sb("strict", [P, P])
        chunked = sb("chunked", [P, P])
        rstd = sb("rstd", [P, 3, S])
        rstd_col = sb("rstd_col", [P, 12])
        small = sb("small", [P, 48])
        biases = sb("biases", [P, 2, P])
        arena = sb("arena", [P, 21504])

        def at(start, *shape):
            n = int(np.prod(shape))
            v = arena[:, start:start + n]
            if len(shape) == 2:
                return v.rearrange("p (a b) -> p a b", b=shape[1])
            return v

        x_stage, mem_stage = at(0, TT, D), at(4096, MT, D)
        vec_stage = at(12288, 3, P)
        mem_t = at(19456, KT, NMEM)
        sq_mem, sq_x = at(16384, KT, NMEM), at(8192, KT, S)
        sq = at(0, KT, S)
        sq_fox = at(18432, 4, S)
        fox_q, fox_k, fox_v, mix_o = at(0, 8, S), at(4096, 4, S), at(6144, TT, S), at(8192, KT, S)
        sq_sb = mix_o[:, 0:4, :]
        mem_k, mem_v = at(12288, KT, NMEM), at(14336, MT, D)
        mem_q = at(0, KT, S)
        prob, prob_t, keep = at(16384, 2, S), at(17408, 2, S), at(18432, 2, S)
        t_buf, r_buf = at(19456, 2, S), at(20480, 2, S)
        stick = at(20480, S + 1)
        f_z, f_a = at(20480, S), at(20992, S)
        neg_c = rstd[:, 2, :]
        conv_u, conv_y, conv_s = at(4096, 4, S + 2), at(6656, 4, S), at(8704, 2, S)
        gm_v, gm_u = at(0, TT, GATE), at(8192, 16, S)
        bs_all, ws_t, ws_sum, ws_stage = at(16384, 8, P), at(17408, 8, P), at(18432, 8, P), at(8192, 8, P)
        lat_q, lat_kv, lat_sq = at(0, 3, S), at(1536, 2, S), at(4096, 5, S)
        mla_q, mla_k, mla_v, mla_qr = at(0, 8, S), at(4096, 8, S), at(8192, TT, 1024), at(12288, 8, S)
        rope_k, rope_t = at(18432, S), at(18944, S)
        ang, turns, pos_i = at(20480, S), at(20992, S), at(6656, S)
        rope_a, rope_b = at(20480, S), at(20992, S)
        y_final, out_stage = at(4096, KT, S), at(8192, TT, D)
        neg_max, row_sum, row_inv = small[:, 0:2], small[:, 2:4], small[:, 4:6]
        eps_t, invf, phase = small[:, 6:7], small[:, 7:8], small[:, 8:9]
        one_col, b_forget = small[:, 9:10], small[:, 10:11]
        ln_mv, ln_std = small[:, 12:20].rearrange("p (t s) -> p t s", s=2), small[:, 20:24]
        ln_part = biases.rearrange("p a b -> p (a b)")[:, 0:24].rearrange("p (c s) -> p c s", s=6)

        bank = [ctx.enter_context(nc.psum_tensor(f"bank{i}", [P, S], F32)) for i in range(8)]
        tile_bank, s_bank, pt_bank, o_bank = bank[0:4], bank[4:6], bank[6], bank[7]
        col_bank, stat_bank = pt_bank, o_bank

        vec_loaded = sem("vec_loaded")
        mem_loaded = sem("mem_loaded")
        x_loaded = sem("x_loaded")
        f_loaded = sem("f_loaded")
        gm_loaded = sem("gm_loaded")
        pos_loaded = sem("pos_loaded")
        consts = sem("consts")
        w_loaded = [sem("w_loaded0"), sem("w_loaded1")]
        w_hi_done = sem("w_hi_done")
        w_split = sem("w_split")
        pool_gate = sem("pool_gate")
        act_gate = sem("act_gate")
        tile_full = sem("tile_full")
        tile_taken = sem("tile_taken")
        vec_t = sem("vec_t")
        hi_done = sem("hi_done")
        h_ready = sem("h_ready")
        g_ready = sem("g_ready")
        sq_done = sem("sq_done")
        acc_ready = sem("acc_ready")
        stat_full = sem("stat_full")
        std_done = sem("std_done")
        own = sem("own")
        act_own = sem("act_own")
        act_out = sem("act_out")
        t_made = sem("t_made")
        s_full = sem("s_full")
        s_masked = sem("s_masked")
        s_taken = sem("s_taken")
        p_ready = sem("p_ready")
        pt_full = sem("pt_full")
        pt_taken = sem("pt_taken")
        pv_done = sem("pv_done")
        o_taken = sem("o_taken")
        c_ready = sem("c_ready")
        gm_ready = sem("gm_ready")
        out_ready = sem("out_ready")
        stored = sem("stored")

        def cols_view(t, slot):
            return t[:, slot, :].rearrange("p (k n) -> p k n", n=COLS)

        def rows_view(t, slot):
            return t[:, slot, :].rearrange("p (k n) -> p k n", k=2)

        def gain(name, i=0):
            c = COLUMN[name] + i
            return vec[:, bass.ds(c, 1)]

        UNITS = [(h, i) for h in range(8) for i in range(TT)]
        MEM_UNITS = [(h, i) for h in range(MEM_HEADS) for i in range(TT)]
        GROUP = {"fox": 2 * TT, "sb": 2 * TT, "mem": 2, "mla": TT}

        def keys(kind, i):
            return NMEM if kind == "mem" else P * (i + 1)

        stream = weight_stream(w)
        block = ctx.enter_context(nc.Block())

        @block.sync
        def _(sp):
            chunk, loads = Count(), [Count(), Count()]
            sp.dma_start(mem_stage, mem_in.rearrange("(t p) n -> p t n", p=P)).then_inc(mem_loaded, 16)
            sp.dma_start(x_stage, x_in.rearrange("(t p) n -> p t n", p=P)).then_inc(x_loaded, 16)

            def load(item, i):
                _, _, parts, _ = item
                slot = chunk.n % 2
                if chunk.n >= 2:
                    sp.wait_ge(w_split, chunk.at(chunk.n - 1))
                for dst, src in parts(raw[:, slot, :], i):
                    sp.dma_start(dst, src).then_inc(w_loaded[slot], 16)
                chunk.n += 1

            for item in stream:
                if item[0] == "tiles":
                    continue
                if item[0] == "loop":
                    with loop(sp, item[1], [(chunk, len(item[2]))]) as i:
                        for part in item[2]:
                            load(part, i)
                else:
                    load(item, 0)
            sp.wait_ge(out_ready, KT)
            sp.dma_start(out.rearrange("(t p) n -> p t n", p=P), out_stage).then_inc(stored, 16)
            sp.wait_ge(stored, 16)

        @block.gpsimd
        def _(pool):
            def in_turn(n, ins):
                ins.then_inc(consts, 1)
                pool.wait_ge(consts, n)

            G = nc.gpsimd
            in_turn(1, G.memset(ident[:], 0.0))
            in_turn(2, G.memset(ones[:], 1.0))
            in_turn(3, G.memset(causal[:], 0.0))
            in_turn(4, G.memset(strict[:], 0.0))
            in_turn(5, G.memset(chunked[:], 0.0))
            in_turn(6, G.memset(eps_t, EPS))
            in_turn(7, G.memset(one_col, 1.0))
            in_turn(8, G.memset(phase[0:64], float(np.pi / 2)))
            in_turn(9, G.memset(phase[64:96], float(np.pi)))
            in_turn(10, G.memset(phase[96:128], 0.0))
            in_turn(11, G.memset(chunked[0:64, 64:128], MASKED))
            in_turn(12, G.affine_select(out=ident[:], in_=ident[:], compare_op=ALU.not_equal, fill=1.0, base=0,
                                        pattern=[[-1, P]], channel_multiplier=1))
            in_turn(13, G.affine_select(out=causal[:], in_=causal[:], compare_op=ALU.is_ge, fill=MASKED, base=0,
                                        pattern=[[-1, P]], channel_multiplier=1))
            in_turn(CONSTANTS, G.affine_select(out=strict[:], in_=strict[:], compare_op=ALU.is_gt, fill=MASKED, base=0,
                                               pattern=[[-1, P]], channel_multiplier=1))
            chunk, tile, loads = Count(), Count(), [Count(), Count()]
            ends = [0, 0]

            def split(item):
                size, tiles, parts, used = item
                slot = chunk.n % 2
                loads[slot].n += len(parts(raw[:, slot, :], 0))
                pool.wait_ge(w_loaded[slot], loads[slot].at(loads[slot].n) * 16)
                if chunk.n >= 2:
                    pool.wait_ge(tile_full, tile.at(ends[0]))
                pool.sem_inc(pool_gate, 1)
                hi, lo, src = w_hi[:, slot, 0:size], w_lo[:, slot, 0:size], raw[:, slot, 0:size]
                one = one_col.to_broadcast([P, size])
                if 0 < used < COLS:
                    hi, lo, src = (t.rearrange("p (k n) -> p k n", n=COLS)[:, :, 0:used] for t in (hi, lo, src))
                    one = one_col.unsqueeze(2).to_broadcast([P, KT, used])
                nc.gpsimd.tensor_tensor(hi, src, one, ALU.mult).then_inc(w_hi_done, 1)
                chunk.n += 1
                pool.wait_ge(w_hi_done, chunk.at(chunk.n))
                nc.gpsimd.tensor_tensor(lo, src, hi.bitcast(F32), ALU.subtract).then_inc(w_split, 1)
                tile.n += tiles
                ends[:] = [ends[1], tile.n]

            for item in stream:
                if item[0] == "tiles":
                    tile.n += item[1]
                elif item[0] == "loop":
                    each, tiles, entry = len(item[2]), sum(c[1] for c in item[2]), list(ends)
                    with loop(pool, item[1], [(chunk, each), (tile, tiles),
                                              (loads[0], each // 2), (loads[1], each // 2)]):
                        for part in item[2]:
                            split(part)
                    assert ends == [e + tiles for e in entry]
                    ends[:] = [e + tiles * item[1] for e in entry]
                else:
                    split(item)

        @block.tensor
        def _(pe):
            chunk, tile, h_n, g_n, stats = Count(), Count(), Count(), Count(), Count()
            unit, group = Count(), Count()

            def wait_chunk():
                pe.wait_ge(w_split, chunk.at(chunk.n + 1))

            def next_bank():
                if tile.n >= 4:
                    pe.wait_ge(tile_taken, tile.at(tile.n - 3))
                return tile_bank[tile.n % 4]

            def full(last):
                last.then_inc(tile_full, 1)
                tile.n += 1

            def split_sum(dst, stationary, moving, arrive=None, part=None):
                n = len(stationary)
                for k in part or range(n):
                    (a_hi, a_lo), (b_hi, b_lo) = stationary[k], moving[k]
                    if arrive is not None:
                        pe.wait_ge(h_ready, arrive + k + 1)
                    nc.tensor.matmul(dst, a_hi, b_hi, start=(k == 0), stop=False)
                    nc.tensor.matmul(dst, a_hi, b_lo, start=False, stop=False)
                    last = nc.tensor.matmul(dst, a_lo, b_hi, start=False, stop=(k == n - 1))
                return last

            def h_tiles(n=KT, first=0, cut=slice(0, S)):
                return [(h_hi[:, first + k, cut], h_lo[:, first + k, cut]) for k in range(n)]

            def mem_tiles(cut=slice(0, NMEM)):
                views = [t[:].rearrange("p a b -> p (a b)").rearrange("p (k n) -> p k n", n=NMEM) for t in (g_hi, g_lo)]
                return [(views[0][:, k, cut], views[1][:, k, cut]) for k in range(KT)]

            def w_tiles(n, cut, view=cols_view):
                slot = chunk.n % 2
                return [(view(w_hi, slot)[:, k, cut], view(w_lo, slot)[:, k, cut]) for k in range(n)]

            def by_feature(tiles=2, moving=None, arrive=None, n_tokens=S):
                wait_chunk()
                for j in range(tiles):
                    dst = next_bank()[:, 0:n_tokens]
                    full(split_sum(dst, w_tiles(KT, slice(P * j, P * j + P)), moving or h_tiles(),
                                   arrive if j == 0 else None))
                chunk.n += 1

            def by_token(pairs=2, stationary=h_tiles, arrive=None):
                wait_chunk()
                for j in range(pairs):
                    b = next_bank()
                    for half in range(2):
                        t = 2 * j + half
                        last = split_sum(b[:, COLS * half:COLS * half + COLS], stationary(cut=slice(P * t, P * t + P)),
                                         w_tiles(KT, slice(0, COLS)), arrive if t == 0 else None)
                    full(last)
                chunk.n += 1

            def back(granule, tiles=range(KT), in_h=False):
                p = granule % 2
                if tiles[0] == 0:
                    wait_chunk()
                    if in_h:
                        pe.wait_ge(h_ready, h_n.n + 2)
                        h_n.n += 2
                    else:
                        pe.wait_ge(g_ready, g_n.at(g_n.n + 2))
                        g_n.n += 2
                moving = h_tiles(2, 2 * granule) if in_h else \
                    [(g_hi[:, 2 * p + k, :], g_lo[:, 2 * p + k, :]) for k in range(2)]
                for n in tiles:
                    dst = next_bank()
                    full(split_sum(dst[:], w_tiles(2, slice(P * n, P * n + P), rows_view), moving))
                if tiles[-1] == KT - 1:
                    chunk.n += 1

            def stat(acc, tokens=S, by_col=False):
                pe.wait_ge(acc_ready, stats.n + 1)
                if group.n:
                    pe.wait_ge(o_taken, group.n)
                if stats.n:
                    pe.wait_ge(std_done, stats.n)
                last = nc.tensor.matmul(stat_bank[:, 0:tokens], ones[:], acc, start=True, stop=True)
                for t in range(tokens // P if by_col else 0):
                    last = nc.tensor.matmul(col_bank[:, t:t + 1], acc[:, P * t:P * t + P], ones[:, 0:1],
                                            start=True, stop=True)
                last.then_inc(stat_full, 1)
                stats.n += 1

            def turn(src, n_tok_tiles, tokens, loaded):
                pe.wait_ge(loaded, 16)
                for n in range(KT):
                    b = next_bank()
                    for t in range(n_tok_tiles):
                        last = nc.tensor.transpose(b[:, P * t:P * t + P], src[:, t, P * n:P * n + P], ident[:])
                    full(last)

            def attention(kind, units, scores, values, n_after=lambda s: None):
                n = len(units)
                per = GROUP[kind]
                first, first_group = unit.n, group.n
                pe.wait_ge(tile_taken, tile.n)
                for s in range(n + 3):
                    if s < n:
                        u = first + s
                        if u >= 2:
                            pe.wait_ge(s_taken, u - 1)
                        h, i = units[s]
                        scores(h, i, s_bank[u % 2][:, 0:keys(kind, i)]).then_inc(s_full, 1)
                    if 0 <= s - 2 < n:
                        u = first + s - 2
                        h, i = units[s - 2]
                        pe.wait_ge(p_ready, u + 1)
                        if u >= 1:
                            pe.wait_ge(pt_taken, u)
                        for k in range(keys(kind, i) // P):
                            last = nc.tensor.transpose(pt_bank[:, P * k:P * k + P],
                                                       prob[:, u % 2, P * k:P * k + P], ident[:])
                        last.then_inc(pt_full, 1)
                    if 0 <= s - 3 < n:
                        u = first + s - 3
                        h, i = units[s - 3]
                        pe.wait_ge(pt_taken, u + 1)
                        if (s - 3) % per == 0:
                            pe.wait_ge(o_taken, first_group + (s - 3) // per)
                        values(h, i, prob_t[:, u % 2, :]).then_inc(pv_done, 1)
                        if (s - 3) % per == per - 1:
                            group.n += 1
                    n_after(s)
                unit.n += n

            def several(ops):
                for j, (dst, a, b, first, last) in enumerate(ops):
                    ins = nc.tensor.matmul(dst, a, b, start=first, stop=last)
                return ins

            pe.wait_ge(consts, CONSTANTS)
            pe.wait_ge(vec_loaded, 16 * sum(len(g) for g in VECTORS))
            for g, rows in enumerate(VECTORS):
                n = sum(r for _, r in rows)
                last = nc.tensor.transpose(s_bank[0][:, P * g:P * g + n], vec_stage[0:n, g, :], ident[0:n, 0:n])
            last.then_inc(vec_t, 1)

            turn(mem_stage, MT, NMEM, mem_loaded)
            turn(x_stage, TT, S, x_loaded)
            stat(sq_mem[:, 0, :], NMEM, by_col=True)
            h_n.n += KT

            def mem_keys(s):
                j, quarter = s % 8 // 4, s % 4
                if s % 8 == 0:
                    wait_chunk()
                dst = next_bank()[:, 0:NMEM] if quarter == 0 else tile_bank[tile.n % 4][:, 0:NMEM]
                last = split_sum(dst, w_tiles(KT, slice(P * j, P * j + P)), mem_tiles(),
                                 part=range(2 * quarter, 2 * quarter + 2))
                if quarter == 3:
                    full(last)
                if s % 8 == 7:
                    chunk.n += 1

            def mem_values_of(s):
                t, half = s % 4 // 2, s % 2
                if s % 4 == 0:
                    wait_chunk()
                b = next_bank() if s % 4 == 0 else tile_bank[tile.n % 4]
                last = split_sum(b[:, COLS * t:COLS * t + COLS], mem_tiles(slice(P * t, P * t + P)),
                                 w_tiles(KT, slice(0, COLS)), part=range(4 * half, 4 * half + 4))
                if s % 4 == 3:
                    full(last)
                    chunk.n += 1

            def fox_scores(h, i, dst):
                q = fox_q[:, h, P * i:P * i + P]
                n = P * (i + 1)
                return several([(dst, q, fox_k[:, h // 2, 0:n], True, False),
                                (dst, ident[:, h:h + 1].to_broadcast([P, P]), neg_c[:, 0:n], False, True)])

            def sb_scores(h, i, dst):
                return several([(dst, fox_q[:, h, P * i:P * i + P], fox_k[:, h // 2, 0:P * (i + 1)], True, True)])

            def head_values(h, i, pt):
                r = HD * (h % 2)
                return several([(o_bank[r:r + HD, P * i:P * i + P], fox_v[:, k, HD * h:HD * h + HD],
                                 pt[:, P * k:P * k + P], k == 0, k == i) for k in range(i + 1)])

            by_feature(arrive=h_n.n)
            h_n.n += KT
            stat(sq_x[:, 0, :], by_col=True)
            for c in range(3):
                by_feature()
            by_feature(1)
            by_token()
            by_token()
            pe.wait_ge(c_ready, 1)
            attention("fox", UNITS, fox_scores, head_values, lambda s: mem_keys(s) if s < 32 else None)
            by_feature()
            stat(sq_fox[:, 0, :])
            for c in range(3):
                by_feature()
            by_token()
            by_token()

            def beside_sb(s):
                if s < 16:
                    mem_values_of(s)
                elif s < 32 and s % 2 == 0:
                    back(0, [(s - 16) // 2], in_h=True)

            attention("sb", UNITS, sb_scores, head_values, beside_sb)

            back(1, range(0, 4), in_h=True)
            stat(sq_sb[:, 0, :])
            back(1, range(4, KT), in_h=True)
            back(2)
            back(3)
            if stop > 1:
                by_feature(arrive=h_n.n)
                h_n.n += KT
                stat(sq[:, 0, :])
                for c in range(3):
                    by_feature()

                def mem_scores(h, i, dst):
                    return several([(dst, mem_q[:, 2 * h + k, P * i:P * i + P], mem_k[:, 2 * h + k, :], k == 0, k == 1)
                                    for k in range(2)])

                def mem_values(h, i, pt):
                    return several([(o_bank[:, 256 * j + P * (i % 2):256 * j + P * (i % 2) + P],
                                     mem_v[:, k, 256 * h + P * j:256 * h + P * j + P], pt[:, P * k:P * k + P],
                                     k == 0, k == 1) for j in range(2) for k in range(2)])

                attention("mem", MEM_UNITS, mem_scores, mem_values,
                          lambda s: back((s - 8) // 4, [s % 4 * 2, s % 4 * 2 + 1]) if s >= 8 else None)
                back(2, [6, 7])
                back(3)
            if stop > 2:
                by_feature(arrive=h_n.n)
                h_n.n += KT
                stat(sq[:, 0, :])
                by_feature()
                for c in range(2):
                    by_feature()
                per = [(chunk, 6), (tile, 24), (g_n, 4)]
                with loop(pe, 4, per):
                    for g in range(2):
                        back(g)
                        by_feature()
                        by_feature()
                back(8)
                by_feature()
                by_feature()
                back(9)
                back(10)
                stat(sq[:, 0, :])
            if stop > 3:
                by_token(arrive=h_n.n)
                h_n.n += KT
                stat(sq[:, 0, :], by_col=True)
                by_token()
                with loop(pe, 3, [(chunk, 2), (tile, 4)]):
                    by_token()
                    by_token()
                pe.wait_ge(gm_loaded, 16 * 2)
                for half in range(2):
                    b = next_bank()
                    for g in range(4):
                        last = nc.tensor.transpose(b[:, P * g:P * g + P], ws_stage[:, 4 * half + g, :], ident[:])
                    full(last)
                for half in range(2):
                    b = next_bank()
                    if half == 0:
                        pe.wait_ge(gm_ready, 1)
                    full(nc.tensor.matmul(b[:], ones[:], ws_t[:, 4 * half:4 * half + 4, :], start=True, stop=True))
                with loop(pe, 4, [(chunk, 2), (tile, 4)]):
                    by_feature()
                    by_feature()

                def spatial(g):
                    for j in range(2):
                        b = next_bank()
                        for t in range(TT):
                            c = 256 * g + P * j
                            last = nc.tensor.matmul(b[:, P * t:P * t + P], gm_v[:, t, c:c + P], ws_t[:, g, :],
                                                    start=True, stop=True)
                        full(last)

                pe.wait_ge(gm_ready, 2)
                spatial(0)
                for g in range(1, 8):
                    spatial(g)
                    back(g - 1)
                back(7)

            def mlp():
                by_feature(arrive=h_n.n)
                h_n.n += KT
                stat(sq[:, 0, :])
                by_feature()
                with loop(pe, 7, [(chunk, 4), (tile, 20), (g_n, 4)]):
                    for g in range(2):
                        back(g)
                        by_feature()
                back(14)
                back(15)

            if stop > 4:
                mlp()
            if stop > 5:
                by_feature(arrive=h_n.n)
                h_n.n += KT
                stat(sq[:, 0, :])
                by_feature(1)
                by_feature(arrive=h_n.n)
                h_n.n += KT
                by_feature(1)
                for a, n, cols in ((0, 3, False), (3, 2, True)):
                    stat(lat_sq[:, a, :], by_col=cols)
                pe.wait_ge(h_ready, h_n.n + 5)
                h_n.n += 5
                for p in range(4):
                    wait_chunk()
                    slot = chunk.n % 2
                    views = [t[:, slot, 0:1536].rearrange("p (k n) -> p k n", n=512) for t in (w_hi, w_lo)]
                    for j in range(4):
                        dst = next_bank()
                        full(split_sum(dst[:], [(views[0][:, k, P * j:P * j + P], views[1][:, k, P * j:P * j + P])
                                                for k in range(3)], h_tiles(3)))
                    chunk.n += 1
                for c in range(2):
                    wait_chunk()
                    for h in range(4):
                        dst = next_bank()
                        full(split_sum(dst[:], w_tiles(2, slice(256 * h, 256 * h + P), rows_view), h_tiles(2, 3)))
                    slot = chunk.n % 2
                    vals = [tuple(rows_view(t, slot)[:, k, :].rearrange("p (h n) -> p h n", n=256)[:, :, P:256]
                                  for t in (w_hi, w_lo)) for k in range(2)]
                    for t in range(TT):
                        dst = next_bank()
                        full(split_sum(dst[:].rearrange("p (h n) -> p h n", n=P),
                                       h_tiles(2, 3, slice(P * t, P * t + P)), vals))
                    chunk.n += 1

                def mla_scores(h, i, dst):
                    n = P * (i + 1)
                    return several([(dst, mla_q[:, h, P * i:P * i + P], mla_k[:, h, 0:n], True, False),
                                    (dst, mla_qr[:, h, P * i:P * i + P], rope_k[:, 0:n], False, True)])

                def mla_values(h, i, pt):
                    return several([(o_bank[:, P * i:P * i + P], mla_v[:, k, P * h:P * h + P],
                                     pt[:, P * k:P * k + P], k == 0, k == i) for k in range(i + 1)])

                attention("mla", UNITS, mla_scores, mla_values,
                          lambda s: back((s - 12) // 8, [(s - 12) % 8]) if s >= 12 else None)
                back(2, [7])
                back(3)
            if stop > 6:
                mlp()
            stat(sq[:, 0, :]) if stop != 3 else None
            for t in range(TT):
                for half in range(2):
                    n_out = 2 * t + half
                    if t == 0:
                        pe.wait_ge(h_ready, h_n.n + 4 * half + 4)
                    if n_out < 4:
                        b = next_bank()
                    else:
                        pe.wait_ge(out_ready, n_out - 3)
                        b = tile_bank[tile.n % 4]
                    for n in range(4):
                        last = nc.tensor.transpose(b[:, P * n:P * n + P],
                                                   y_final[:, 4 * half + n, P * t:P * t + P], ident[:])
                    full(last)

        @block.vector
        def _(dve):
            V = nc.vector
            tile, hi_n, g_n, h_n, mine, stats, acts, made = (Count() for _ in range(8))
            sq_n, unit, group = Count(), Count(), Count()

            def keep_order(ins):
                ins.then_inc(own, 1)
                mine.n += 1

            def settle():
                dve.wait_ge(own, mine.at(mine.n))

            def take(fn):
                dve.wait_ge(tile_full, tile.at(tile.n + 1))
                b = tile_bank[tile.n % 4]
                fn(b).then_inc(tile_taken, 1)
                tile.n += 1

            def low_half(lo, hi, src, scale, ready):
                dve.wait_ge(hi_done, hi_n.at(hi_n.n + 1))
                hi_n.n += 1
                if scale is None:
                    V.tensor_tensor(lo, src, hi.bitcast(F32), ALU.subtract).then_inc(ready, 1)
                else:
                    V.scalar_tensor_tensor(lo, src, scale, hi.bitcast(F32), ALU.mult, ALU.subtract).then_inc(ready, 1)

            def lo_h(n, name):
                low_half(h_lo[:, n, :], h_hi[:, n, :], x[:, n, :], gain(name, n), h_ready)

            def lo_g(granule, j, src):
                p = 2 * (granule % 2) + j
                low_half(g_lo[:, p, :], g_hi[:, p, :], src, None, g_ready)
                g_n.n += 1

            def lows_done():
                if g_n.n:
                    dve.wait_ge(g_ready, g_n.at(g_n.n))

            def sum_squares(s, n_tiles):
                sq_n.n += n_tiles
                dve.wait_ge(sq_done, sq_n.n)
                n = n_tiles
                while n > 1:
                    m = n // 2
                    ins = V.tensor_tensor(s[:, 0:m, :], s[:, 0:m, :], s[:, n - m:n, :], ALU.add)
                    n -= m
                    if n > 1:
                        keep_order(ins)
                        settle()
                ins.then_inc(acc_ready, 1)

            def finish_rstd(row, col=None):
                stats.n += 1
                dve.wait_ge(std_done, stats.n)
                ins = V.reciprocal(row, row)
                if col is not None:
                    keep_order(ins)
                    ins = V.reciprocal(col, col)
                keep_order(ins)
                settle()

            def back_tile(n):
                take(lambda b: V.tensor_tensor(x[:, n, :], b[:], x[:, n, :], ALU.add))

            def back(last=None):
                for n in range(KT):
                    back_tile(n)
                    if last and n >= 1:
                        lo_h(n - 1, last)
                if last:
                    lo_h(KT - 1, last)

            def scaled(dst, by, factor=None):
                def fn(b):
                    if factor is None:
                        return V.tensor_tensor(dst, b[:], by, ALU.mult)
                    return V.scalar_tensor_tensor(dst, b[:], factor, by, ALU.mult, ALU.mult)
                return fn

            def attention(kind, units, mask, out_group, between):
                n, per = len(units), GROUP[kind]
                first = unit.n
                for s in range(n + 4):
                    if 0 <= s - 2 < n:
                        u = first + s - 2
                        h, i = units[s - 2]
                        nk = keys(kind, i)
                        dve.wait_ge(s_taken, u + 1)
                        if kind == "sb":
                            dve.wait_ge(p_ready, u)
                            k_rev = keep[:, u % 2, 0:nk][:, ::-1]
                            keep_order(V.tensor_tensor_scan(stick[:, S - nk:S][:, ::-1], k_rev, k_rev, 1.0,
                                                            ALU.mult, ALU.min))
                            settle()
                            V.tensor_tensor(prob[:, u % 2, 0:nk], prob[:, u % 2, 0:nk],
                                            stick[:, S - nk + 1:S + 1], ALU.mult).then_inc(p_ready, 1)
                        else:
                            keep_order(V.reciprocal(row_inv[:, u % 2:u % 2 + 1], row_sum[:, u % 2:u % 2 + 1]))
                            settle()
                            V.tensor_scalar(prob[:, u % 2, 0:nk], prob[:, u % 2, 0:nk],
                                            row_inv[:, u % 2:u % 2 + 1], None, ALU.mult).then_inc(p_ready, 1)
                    between(s)
                    if s < n:
                        u = first + s
                        h, i = units[s]
                        nk = keys(kind, i)
                        b = s_bank[u % 2]
                        dve.wait_ge(s_full, u + 1)
                        if mask is not None:
                            ins = V.tensor_tensor(b[:, nk - P:nk], b[:, nk - P:nk], mask[:], ALU.add)
                            if kind != "sb":
                                keep_order(ins)
                                settle()
                        if kind != "sb":
                            ins = V.tensor_reduce(neg_max[:, u % 2:u % 2 + 1], b[:, 0:nk], AX.X, ALU.max, negate=True)
                        ins.then_inc(s_masked, 1)
                    if 0 <= s - 3 < n and (s - 3) % per == per - 1:
                        dve.wait_ge(pv_done, first + s - 3 + 1)
                        out_group((s - 3) // per, o_bank)
                        group.n += 1
                unit.n += n

            dve.wait_ge(vec_t, 1)
            keep_order(V.tensor_copy(vec[:], s_bank[0][:, 0:NVEC]))
            settle()
            for n in range(KT):
                take(lambda b: V.tensor_copy(mem_t[:, n, :], b[:, 0:NMEM]))
            m_hi, m_lo = (t[:].rearrange("p a b -> p (a b)").rearrange("p (k n) -> p k n", n=NMEM) for t in (g_hi, g_lo))
            for n in range(KT):
                low_half(m_lo[:, n, :], m_hi[:, n, :], mem_t[:, n, :], gain("mem_norm_g", n), h_ready)
            sum_squares(sq_mem, KT)
            for n in range(KT):
                take(lambda b: V.tensor_copy(x[:, n, :], b[:]))
            for n in range(KT):
                lo_h(n, "attn_norm_g")
            sum_squares(sq_x, KT)
            finish_rstd(rstd[:, 1, 0:NMEM], rstd_col[:, 4:6])

            def mem_keys(n):
                take(lambda b: V.tensor_tensor(mem_k[:, n, :], b[:, 0:NMEM], rstd[:, 1, 0:NMEM], ALU.mult))

            def mem_values_of(c):
                def two_tokens(b):
                    for t in range(MT):
                        last = V.tensor_scalar(mem_v[:, t, COLS * c:COLS * c + COLS], b[:, COLS * t:COLS * t + COLS],
                                               rstd_col[:, 4 + t:5 + t], None, ALU.mult)
                    return last
                take(two_tokens)

            def head_inputs():
                for n in range(4):
                    def two_heads(b):
                        for j in range(2):
                            r = slice(HD * j, HD * j + HD)
                            last = V.scalar_tensor_tensor(fox_q[r, 2 * n + j, :], b[r, :], HD ** -0.5, rstd[r, 0, :],
                                                          ALU.mult, ALU.mult)
                        return last
                    take(two_heads)
                for n in range(4):
                    take(scaled(fox_k[:, n, :], rstd[:, 0, :]))

            def head_values():
                for c in range(2):
                    for j in range(2):
                        def two_tokens(b):
                            for half in range(2):
                                t = 2 * j + half
                                last = V.tensor_scalar(fox_v[:, t, COLS * c:COLS * c + COLS],
                                                       b[:, COLS * half:COLS * half + COLS], rstd_col[:, t:t + 1],
                                                       None, ALU.mult)
                            return last
                        take(two_tokens)

            finish_rstd(rstd[:, 0, :], rstd_col[:, 0:4])
            for n in range(8):
                r = slice(HD, P) if n % 2 == 0 else slice(0, HD)
                V.memset(fox_q[r, n, :], 0.0)
            head_inputs()
            keep_order(V.memset(neg_c[:], 0.0))
            take(lambda b: V.tensor_tensor(f_z[0:8, :], b[0:8, :], rstd[0:8, 0, :], ALU.mult))
            dve.wait_ge(tile_taken, tile.n)
            dve.wait_ge(f_loaded, 16)
            V.tensor_scalar(f_z[0:8, :], f_z[0:8, :], b_forget[0:8], None, ALU.add).then_inc(t_made, 1)
            made.n += 1
            head_values()
            acts.n += 1
            dve.wait_ge(act_out, acts.n)
            keep_order(V.tensor_scalar(f_z[0:8, :], f_z[0:8, :], 0.0, None, ALU.min))
            settle()
            keep_order(V.tensor_tensor(f_a[0:8, :], f_a[0:8, :], f_z[0:8, :], ALU.subtract))
            settle()
            V.tensor_tensor_scan(neg_c[0:8, :], one_col[0:8].to_broadcast([8, S]), f_a[0:8, :], 0.0,
                                 ALU.mult, ALU.add).then_inc(c_ready, 1)

            def out_to(first_tile):
                def fn(g, b):
                    V.tensor_copy(mix_o[:, first_tile + g, :], b[:]).then_inc(o_taken, 1)
                return fn

            def normed(n):
                name, row, i = ("fox_out_g", 2, n) if n < 4 else ("sb_out_g", 1, n - 4)
                V.scalar_tensor_tensor(mix_o[:, n, :], mix_o[:, n, :], gain(name, i), rstd[:, row, :],
                                       ALU.mult, ALU.mult).then_inc(t_made, 1)
                made.n += 1

            attention("fox", UNITS, causal, out_to(0),
                      lambda s: mem_keys(s // 4 - 1) if s and s % 4 == 0 and s <= 32 else None)
            sum_squares(sq_fox, 4)
            head_inputs()
            finish_rstd(rstd[:, 2, :])
            head_values()
            keep_order(V.memset(stick[:, S:S + 1], 1.0))
            settle()

            def beside_sb(s):
                if s < 4:
                    normed(s)
                elif 6 <= s < 10:
                    n = s - 6
                    low_half(h_lo[:, n, :], h_hi[:, n, :], mix_o[:, n, :], None, h_ready)
                if s in (4, 8, 12, 16):
                    mem_values_of(s // 4 - 1)
                elif 16 < s < 32 and s % 2:
                    back_tile((s - 17) // 2)

            attention("sb", UNITS, strict, out_to(4), beside_sb)

            sum_squares(sq_sb, 4)
            for n in range(4):
                back_tile(n)
            finish_rstd(rstd[:, 1, :])
            for j in range(2):
                normed(4 + j)
                back_tile(4 + j)
            for j in range(2):
                lo_g(2, j, mix_o[:, 4 + j, :])
                back_tile(6 + j)
            for j in range(2):
                normed(6 + j)
            back_tile(0)
            for j in range(2):
                lo_g(3, j, mix_o[:, 6 + j, :])
            for n in range(1, KT):
                back_tile(n)
            back("xattn_norm_g" if stop > 1 else None)
            if stop > 1:
                sum_squares(sq, KT)
                finish_rstd(rstd[:, 0, :])
                for n in range(KT):
                    take(scaled(mem_q[:, n, :], rstd[:, 0, :], 256 ** -0.5))

                def mem_group(g, b):
                    lows_done()
                    V.tensor_copy(t_buf[:, :, 256 * (g % 2):256 * (g % 2) + 256],
                                  b[:].rearrange("p (j n) -> p j n", j=2)).then_inc(o_taken, 1)
                    if g % 2:
                        for j in range(2):
                            lo_g(g // 2, j, t_buf[:, j, :])

                attention("mem", MEM_UNITS, None, mem_group,
                          lambda s: [back_tile(2 * (s - 9) % 8 + j) for j in range(2)] if 9 <= s < 20 else None)
                for n in (6, 7):
                    back_tile(n)
                back("ffn_norm_g" if stop > 2 else None)
            if stop > 2:
                V.memset(conv_u[:, :, 0:2], 0.0)
                sum_squares(sq, KT)
                finish_rstd(rstd[:, 0, :])

                def take_up():
                    for j in range(4):
                        take(lambda b: V.tensor_tensor(conv_u[:, j, 2:], b[:], rstd[:, 0, :], ALU.mult))

                def gated(granule, g_reg=0, stride=0, between=lambda: None):
                    def w_col(name, j):
                        return gain(name, g_reg * stride + 2 * granule + (j % 2) + 22 * (j // 2))
                    for j in range(4):
                        acts.n += 1
                        dve.wait_ge(act_out, acts.at(acts.n))
                        keep_order(V.scalar_tensor_tensor(conv_y[:, j, :], conv_u[:, j, 1:S + 1], w_col("conv_w1", j),
                                                          conv_y[:, j, :], ALU.mult, ALU.add))
                        if j % 2:
                            between()
                    for j in range(4):
                        dve.wait_ge(own, mine.at(mine.n - 3 + j))
                        V.scalar_tensor_tensor(conv_y[:, j, :], conv_u[:, j, 0:S], w_col("conv_w0", j),
                                               conv_y[:, j, :], ALU.mult, ALU.add).then_inc(t_made, 1)
                        made.n += 1
                        if j % 2:
                            between()
                    dve.wait_ge(t_made, made.at(made.n))
                    lows_done()
                    for j in range(2):
                        acts.n += 1
                        dve.wait_ge(act_out, acts.at(acts.n))
                        V.tensor_tensor(t_buf[:, j, :], conv_s[:, j, :], conv_y[:, 2 + j, :], ALU.mult).then_inc(t_made, 1)
                        made.n += 1
                        between()
                    dve.wait_ge(t_made, made.at(made.n))
                    for j in range(2):
                        lo_g(granule, j, t_buf[:, j, :])
                        between()

                def gated_and_back(granule, g_reg=0, stride=0):
                    n = iter(range(KT))
                    gated(granule, g_reg, stride, lambda: back_tile(next(n)))

                take_up()
                gated(0)
                take_up()
                with loop(dve, 4, [(tile, 24), (hi_n, 4), (g_n, 4), (mine, 8), (acts, 12), (made, 12)]) as i:
                    for g in range(2):
                        gated_and_back(1 + g, i, 4)
                        take_up()
                gated_and_back(9)
                take_up()
                gated_and_back(10)
                back()
                sum_squares(sq, KT)
                finish_rstd(rstd[:, 0, :])
            if stop > 3:
                for n in range(KT):
                    V.scalar_tensor_tensor(x[:, n, :], x[:, n, :], gain("final_norm_g", n), rstd[:, 0, :],
                                           ALU.mult, ALU.mult).then_inc(t_made, 1)
                    made.n += 1
                    if n:
                        lo_h(n - 1, "mix0")
                lo_h(KT - 1, "mix0")
                sum_squares(sq, KT)
                finish_rstd(rstd[:, 0, :], rstd_col[:, 0:4])

                def gate_values(c, reg=0, stride=0):
                    for j in range(2):
                        def two_tokens(b):
                            for half in range(2):
                                t = 2 * j + half
                                last = V.tensor_scalar(gm_v[:, t, bass.ds(reg * stride + COLS * c, COLS)],
                                                       b[:, COLS * half:COLS * half + COLS], rstd_col[:, t:t + 1],
                                                       None, ALU.mult)
                            return last
                        take(two_tokens)

                with loop(dve, 4, [(tile, 4)]) as i:
                    gate_values(0, i, 512)
                    gate_values(1, i, 512)
                for half in range(2):
                    take(lambda b: V.tensor_copy(ws_t[:, 4 * half:4 * half + 4, :], b[:].rearrange("p (g n) -> p g n", n=P)))
                dve.wait_ge(tile_taken, tile.n)
                V.memset(ws_t[64:128, :, 0:64], 0.0).then_inc(gm_ready, 1)
                for half in range(2):
                    take(lambda b: V.tensor_copy(ws_sum[:, 4 * half:4 * half + 4, :], b[:].rearrange("p (g n) -> p g n", n=P)))
                acts.n += 16
                dve.wait_ge(act_out, acts.n)
                for t in range(TT):
                    for c in range(4):
                        keep_order(V.bn_stats(ln_part[:, c, :], gm_v[:, t, 512 * c:512 * c + 512]))
                    settle()
                    keep_order(V.bn_aggr(ln_mv[:, t, :], ln_part[:]))
                    settle()
                V.tensor_copy(ln_std, ln_mv[:, :, 1]).then_inc(t_made, 1)
                made.n += 1
                for n in range(0, 2):
                    take(scaled(gm_u[:, n, :], rstd[:, 0, :]))
                acts.n += 1
                dve.wait_ge(act_out, acts.n)
                keep_order(V.reciprocal(ln_std, ln_std))
                settle()
                for t in range(TT):
                    ins = V.tensor_scalar(gm_v[:, t, :], gm_v[:, t, :], ln_mv[:, t, 0:1], ln_std[:, t:t + 1],
                                          ALU.subtract, ALU.mult)
                ins.then_inc(gm_ready, 1)
                for n in range(2, 16):
                    take(scaled(gm_u[:, n, :], rstd[:, 0, :]))

                def gated(g):
                    for j in range(2):
                        c = 2 * g + j
                        keep_order(V.scalar_tensor_tensor(biases[:, j, :], ws_sum[:, g, :], gain("a_ln_v_b_2", c),
                                                          bs_all[:, g, :], ALU.mult, ALU.add))
                    settle()
                    for j in range(2):
                        c = 2 * g + j
                        take(lambda b: V.scalar_tensor_tensor(
                            r_buf[:, j, :].rearrange("p (t n) -> p t n", n=P), b[:].rearrange("p (t n) -> p t n", n=P),
                            gain("a_ln_v_g_2", c), biases[:, j:j + 1, :].to_broadcast([P, TT, P]), ALU.mult, ALU.add))
                    acts.n += 2
                    dve.wait_ge(act_out, acts.n)
                    lows_done()
                    for j in range(2):
                        dve.wait_ge(tile_taken, tile.n - 1 + j)
                        V.tensor_tensor(t_buf[:, j, :], r_buf[:, j, :], gm_u[:, 2 * g + j, :], ALU.mult).then_inc(t_made, 1)
                        made.n += 1
                    dve.wait_ge(t_made, made.n)
                    for j in range(2):
                        lo_g(g, j, t_buf[:, j, :])

                gated(0)
                for g in range(1, 8):
                    gated(g)
                    back()
                back("mlp0" if stop > 4 else None)

            def mlp(following):
                sum_squares(sq, KT)
                finish_rstd(rstd[:, 0, :])

                def up(granule):
                    for j in range(2):
                        take(lambda b: V.scalar_tensor_tensor(r_buf[:, j, :], b[:], 0.0, rstd[:, 0, :],
                                                              ALU.max, ALU.mult))
                    for j in range(2):
                        lo_g(granule, j, t_buf[:, j, :])

                up(0)
                up(1)
                with loop(dve, 7, [(tile, 20), (hi_n, 4), (g_n, 4)]):
                    for g in range(2):
                        back()
                        up(g)
                back()
                back(following)

            if stop > 4:
                mlp("mix1" if stop > 5 else None)
            if stop > 5:
                sum_squares(sq, KT)
                finish_rstd(rstd[:, 0, :])
                for n in range(3):
                    take(scaled(lat_q[:, n, :], rstd[:, 0, :]))
                for n in range(KT):
                    lo_h(n, "kv_src_norm_g_2")
                dve.wait_ge(pos_loaded, 32)
                keep_order(V.tensor_copy(ang, pos_i.bitcast(I32)))
                settle()
                keep_order(V.tensor_scalar(ang, ang, invf, None, ALU.mult))
                settle()
                keep_order(V.tensor_scalar(turns, ang, 1.0 / (2 * np.pi), 12582912.0, ALU.mult, ALU.add))
                settle()
                keep_order(V.tensor_scalar(turns, turns, 12582912.0, None, ALU.subtract))
                settle()
                c1 = 6.28125
                c2 = 0.0019350051879882812
                c3 = 2 * np.pi - c1 - c2
                for c in (c1, c2, c3):
                    keep_order(V.scalar_tensor_tensor(ang, turns, -c, ang, ALU.mult, ALU.add))
                    settle()
                keep_order(V.tensor_scalar(ang, ang, phase, None, ALU.add))
                settle()
                keep_order(V.tensor_scalar(turns, ang, float(np.pi), -2 * np.pi, ALU.is_gt, ALU.mult))
                settle()
                keep_order(V.tensor_tensor(ang, ang, turns, ALU.add))
                settle()
                V.tensor_scalar(ang, ang, 3.1415925, -3.1415925, ALU.min, ALU.max).then_inc(t_made, 1)
                made.n += 1
                for n in range(2):
                    take(scaled(lat_kv[:, n, :], rstd[:, 0, :]))
                acts.n += 1
                dve.wait_ge(act_out, acts.n)
                keep_order(V.memset(rope_k[:], 0.0))
                settle()

                def turned(b):
                    V.tensor_tensor(rope_a[0:64, :], b[0:64, :], rope_t[0:64, :], ALU.mult)
                    return V.tensor_tensor(rope_b[0:64, :], b[64:128, :], rope_t[64:128, :], ALU.mult)

                take(lambda b: turned(b))
                dve.wait_ge(tile_taken, tile.n)
                keep_order(V.tensor_tensor(rope_a[0:64, :], rope_a[0:64, :], rope_b[0:64, :], ALU.add))
                settle()
                keep_order(V.tensor_tensor(rope_k[0:64, :], rope_a[0:64, :], rstd[0:64, 0, :], ALU.mult))
                sum_squares(lat_sq[:, 0:3, :], 3)
                sum_squares(lat_sq[:, 3:5, :], 2)
                for n in range(3):
                    low_half(h_lo[:, n, :], h_hi[:, n, :], lat_q[:, n, :], gain("b_q_norm_g_2", n), h_ready)
                for n in range(2):
                    low_half(h_lo[:, 3 + n, :], h_hi[:, 3 + n, :], lat_kv[:, n, :], gain("kv_a_norm_g_2", n), h_ready)
                finish_rstd(rstd[:, 1, :])
                finish_rstd(rstd[:, 2, :], rstd_col[:, 8:12])
                scale = (NOPE + ROPE) ** -0.5
                V.memset(mla_qr[64:128, :, :], 0.0)
                for h in range(MLA_HEADS):
                    take(scaled(mla_q[:, h, :], rstd[:, 1, :], scale))
                    settle()
                    take(lambda b: turned(b))
                    dve.wait_ge(tile_taken, tile.n)
                    keep_order(V.tensor_tensor(rope_a[0:64, :], rope_a[0:64, :], rope_b[0:64, :], ALU.add))
                    settle()
                    keep_order(V.scalar_tensor_tensor(mla_qr[0:64, h, :], rope_a[0:64, :], scale, rstd[0:64, 1, :],
                                                      ALU.mult, ALU.mult))
                for c in range(2):
                    for h in range(4):
                        take(scaled(mla_k[:, 4 * c + h, :], rstd[:, 2, :]))
                    for t in range(TT):
                        take(lambda b: V.tensor_scalar(mla_v[:, t, 512 * c:512 * c + 512], b[:],
                                                       rstd_col[:, 8 + t:9 + t], None, ALU.mult))

                def mla_group(g, b):
                    lows_done()
                    V.tensor_copy(t_buf[:, g % 2, :], b[:]).then_inc(o_taken, 1)
                    if g % 2:
                        for j in range(2):
                            lo_g(g // 2, j, t_buf[:, j, :])

                attention("mla", UNITS, chunked, mla_group,
                          lambda s: back_tile((s - 13) % 8) if 13 <= s else None)
                back_tile(7)
                back("mlp1" if stop > 6 else None)
            if stop > 6:
                mlp(None)

            if stop != 3:
                sum_squares(sq, KT)
                finish_rstd(rstd[:, 0, :])
            for n in range(KT):
                if stop == 99:
                    V.scalar_tensor_tensor(y_final[:, n, :], x[:, n, :], gain("final_norm_g_2", n), rstd[:, 0, :],
                                           ALU.mult, ALU.mult).then_inc(h_ready, 1)
                else:
                    V.tensor_copy(y_final[:, n, :], x[:, n, :]).then_inc(h_ready, 1)
            for t in range(TT):
                for half in range(2):
                    dve.wait_ge(tile_full, tile.n + 1)
                    b = tile_bank[tile.n % 4]
                    V.tensor_copy(out_stage[:, t, 512 * half:512 * half + 512], b[:]).then_inc(out_ready, 1)
                    tile.n += 1

        @block.scalar
        def _(act):
            A = nc.scalar.activation
            tile, hi_n, g_n, made, stats, acts, mine = (Count() for _ in range(7))
            sq_n, unit, group = Count(), Count(), Count()

            for g, rows in enumerate(VECTORS):
                r = 0
                for name, n in rows:
                    act.dma_start(vec_stage[r:r + n, g, :], w[name].rearrange("(r p) -> r p", p=P)).then_inc(vec_loaded, 16)
                    r += n
            act.dma_start(b_forget[0:8], w["b_forget"].rearrange("(p a) -> p a", a=1)).then_inc(f_loaded, 16)
            act.dma_start(invf, freq[:] if not hasattr(freq, "ap") else freq.ap()).then_inc(pos_loaded, 16)
            act.wait_ge(consts, CONSTANTS)

            def taken(n=1):
                tile.n += n
                act.wait_ge(tile_taken, tile.at(tile.n))

            def squares(s, n, src):
                A(s[:, n, :], src, ACT.Square).then_inc(sq_done, 1)
                sq_n.n += 1

            def high_half(dst, src, scale=1.0):
                A(dst, src, ACT.Copy, scale=scale).then_inc(hi_done, 1)
                hi_n.n += 1

            def prep(n, name, s=None):
                if name:
                    high_half(h_hi[:, n, :], x[:, n, :], gain(name, n))
                squares(sq if s is None else s, n, x[:, n, :])

            def root(row, col, row_src, col_src, width):
                stats.n += 1
                act.wait_ge(stat_full, stats.n)
                ins = A(row, row_src, ACT.Sqrt, scale=1.0 / width, bias=eps_t)
                if col is not None:
                    ins = A(col, col_src, ACT.Sqrt, scale=1.0 / width, bias=eps_t)
                ins.then_inc(std_done, 1)

            def back(last=False, name=None):
                if not last:
                    tile.n += KT
                    return
                for n in range(KT):
                    taken()
                    prep(n, name)

            def hi_g(granule, from_t=True):
                for j in range(2):
                    if from_t:
                        made.n += 1
                        act.wait_ge(t_made, made.at(made.n))
                    act.sem_inc(act_gate, 1)
                    high_half(g_hi[:, 2 * (granule % 2) + j, :], t_buf[:, j, :])

            def attention(kind, units, n_after=lambda s: None, n_group=lambda g: None):
                n, per = len(units), GROUP[kind]
                first = unit.n
                for s in range(n + 4):
                    if 0 <= s - 2 < n:
                        u = first + s - 2
                        h, i = units[s - 2]
                        nk = keys(kind, i)
                        act.wait_ge(pt_full, u + 1)
                        if u >= 2:
                            act.wait_ge(pv_done, u - 1)
                        A(prob_t[:, u % 2, 0:nk], pt_bank[:, 0:nk], ACT.Copy).then_inc(pt_taken, 1)
                    if s < n:
                        u = first + s
                        h, i = units[s]
                        nk = keys(kind, i)
                        act.wait_ge(s_masked, u + 1)
                        if u >= 2:
                            act.wait_ge(pt_full, u - 1)
                        src, dst = s_bank[u % 2][:, 0:nk], prob[:, u % 2, 0:nk]
                        if kind == "sb":
                            A(dst, src, ACT.Sigmoid)
                            A(keep[:, u % 2, 0:nk], src, ACT.Sigmoid, scale=-1.0).then_inc(s_taken, 1)
                        else:
                            A(dst, src, ACT.Exp, bias=neg_max[:, u % 2:u % 2 + 1],
                              accum_out=row_sum[:, u % 2:u % 2 + 1]).then_inc(s_taken, 1)
                    if 0 <= s - 3 < n and (s - 3) % per == per - 1:
                        n_group((s - 3) // per)
                    n_after(s)
                unit.n += n

            m_hi = g_hi[:].rearrange("p a b -> p (a b)").rearrange("p (k n) -> p k n", n=NMEM)
            act.wait_ge(own, 1)
            for n in range(KT):
                taken()
                high_half(m_hi[:, n, :], mem_t[:, n, :], gain("mem_norm_g", n))
                squares(sq_mem, n, mem_t[:, n, :])
            for n in range(KT):
                taken()
                prep(n, "attn_norm_g", sq_x)
            root(rstd[:, 1, 0:NMEM], rstd_col[:, 4:6], stat_bank[:, 0:NMEM], col_bank[:, 0:2], D)
            root(rstd[:, 0, :], rstd_col[:, 0:4], stat_bank[:], col_bank[:, 0:4], D)
            tile.n += 8 + 1
            made.n += 1
            act.wait_ge(t_made, made.n)
            A(f_a[0:8, :], f_z[0:8, :], ACT.Abs).then_inc(act_own, 1)
            act.wait_ge(act_own, 1)
            A(f_a[0:8, :], f_a[0:8, :], ACT.Exp, scale=-1.0).then_inc(act_own, 1)
            act.wait_ge(act_own, 2)
            A(f_a[0:8, :], f_a[0:8, :], ACT.Ln, bias=one_col[0:8]).then_inc(act_out, 1)
            acts.n += 1
            tile.n += 4
            def squares_of_group(s, first_tile):
                def fn(g):
                    act.wait_ge(o_taken, first_tile + g + 1)
                    if first_tile:
                        act.wait_ge(h_ready, 2 * KT + g + 1)
                    squares(s, g, mix_o[:, first_tile + g, :])
                return fn

            def fox_halves(s):
                if 4 <= s < 8:
                    made.n += 1
                    act.wait_ge(t_made, made.n)
                    high_half(h_hi[:, s - 4, :], mix_o[:, s - 4, :])

            attention("fox", UNITS, n_group=squares_of_group(sq_fox, 0))
            tile.n += 8
            root(rstd[:, 2, :], None, stat_bank[:], None, 512)
            tile.n += 12
            act.wait_ge(tile_taken, tile.n)
            attention("sb", UNITS, fox_halves, squares_of_group(sq_sb, 4))
            tile.n += 4 + 8
            act.wait_ge(tile_taken, tile.n)
            root(rstd[:, 1, :], None, stat_bank[:], None, 512)
            for n in range(4):
                made.n += 1
                act.wait_ge(t_made, made.n)
                high_half(g_hi[:, n, :], mix_o[:, 4 + n, :])
            tile.n += 16
            back(True, "xattn_norm_g" if stop > 1 else None)
            if stop > 1:
                root(rstd[:, 0, :], None, stat_bank[:], None, D)
                tile.n += 8
                start_tile, start_group = tile.n, 8

                def mem_split(g):
                    if g % 2:
                        act.wait_ge(o_taken, start_group + g + 1)
                        if g // 2 >= 2:
                            act.wait_ge(tile_full, start_tile + 8 * (g // 2 - 1))
                        hi_g(g // 2, from_t=False)
                attention("mem", MEM_UNITS, n_group=mem_split)
                tile.n += 24
                back(True, "ffn_norm_g" if stop > 2 else None)
            if stop > 2:
                root(rstd[:, 0, :], None, stat_bank[:], None, D)

                def up(granule, g_reg=0, stride=0):
                    for j in range(4):
                        taken()
                        act.sem_inc(act_gate, 1)
                        c = g_reg * stride + 2 * granule + (j % 2) + 22 * (j // 2)
                        A(conv_y[:, j, :], conv_u[:, j, 2:], ACT.Identity, scale=gain("conv_w2", c),
                          bias=gain("conv_b", c)).then_inc(act_out, 1)
                        acts.n += 1
                    made.n += 4
                    for j in range(2):
                        act.wait_ge(t_made, made.at(made.n - 3 + j))
                        A(conv_s[:, j, :], conv_y[:, j, :], ACT.Silu).then_inc(act_out, 1)
                        acts.n += 1
                    hi_g(granule)

                up(0)
                up(1)
                with loop(act, 4, [(tile, 24), (hi_n, 4), (acts, 12), (made, 12)]) as i:
                    for g in range(2):
                        back()
                        up(2 + g, i, 4)
                back()
                up(10)
                if stop > 3:
                    act.dma_start(ws_stage, w["a_w_s_2"].rearrange("g i j -> i g j")).then_inc(gm_loaded, 16)
                    act.dma_start(bs_all, w["a_b_s_2"].partition_broadcast(P)).then_inc(gm_loaded, 16)
                back()
                back(True, None)
                root(rstd[:, 0, :], None, stat_bank[:], None, D)
            if stop > 3:
                for n in range(KT):
                    made.n += 1
                    act.wait_ge(t_made, made.n)
                    prep(n, "mix0")
                root(rstd[:, 0, :], rstd_col[:, 0:4], stat_bank[:], col_bank[:, 0:4], D)
                with loop(act, 4, [(tile, 4), (acts, 4)]) as i:
                    for c in range(2):
                        for j in range(2):
                            taken()
                            act.sem_inc(act_gate, 1)
                            v = gm_v[:, 2 * j:2 * j + 2, bass.ds(i * 512 + COLS * c, COLS)]
                            A(v, v, ACT.Gelu).then_inc(act_out, 1)
                            acts.n += 1
                tile.n += 4
                for n in range(2):
                    taken()
                made.n += 1
                act.wait_ge(t_made, made.n)
                A(ln_std, ln_std, ACT.Sqrt, bias=eps_t).then_inc(act_out, 1)
                acts.n += 1
                for n in range(16):
                    if n >= 2:
                        taken()
                    A(gm_u[:, n, :], gm_u[:, n, :], ACT.Gelu).then_inc(act_out, 1)
                    acts.n += 1
                for g in range(8):
                    tile.n += 2
                    hi_g(g)
                    if g >= 1:
                        back()
                back(True, "mlp0" if stop > 4 else None)

            def mlp(following):
                root(rstd[:, 0, :], None, stat_bank[:], None, D)

                def up(granule):
                    for j in range(2):
                        taken()
                        act.sem_inc(act_gate, 1)
                        A(t_buf[:, j, :], r_buf[:, j, :], ACT.Square)
                        A(g_hi[:, 2 * (granule % 2) + j, :], r_buf[:, j, :], ACT.Square).then_inc(hi_done, 1)
                        hi_n.n += 1

                up(0)
                up(1)
                with loop(act, 7, [(tile, 20), (hi_n, 4)]):
                    for g in range(2):
                        back()
                        up(g)
                back()
                back(True, following)

            if stop > 4:
                mlp("mix1" if stop > 5 else None)
            if stop > 5:
                root(rstd[:, 0, :], None, stat_bank[:], None, D)
                taken(3)
                act.dma_start(pos_i.bitcast(I32), w["positions_2"].partition_broadcast(P)).then_inc(pos_loaded, 16)
                for n in range(KT):
                    high_half(h_hi[:, n, :], x[:, n, :], gain("kv_src_norm_g_2", n))
                for n in range(3):
                    squares(lat_sq, n, lat_q[:, n, :])
                made.n += 1
                act.wait_ge(t_made, made.n)
                A(rope_t[:], ang, ACT.Sin).then_inc(act_out, 1)
                acts.n += 1
                for n in range(2):
                    taken()
                    squares(lat_sq, 3 + n, lat_kv[:, n, :])
                taken()
                for n in range(3):
                    high_half(h_hi[:, n, :], lat_q[:, n, :], gain("b_q_norm_g_2", n))
                for n in range(2):
                    high_half(h_hi[:, 3 + n, :], lat_kv[:, n, :], gain("kv_a_norm_g_2", n))
                root(rstd[:, 1, :], None, stat_bank[:], None, Q_LORA)
                root(rstd[:, 2, :], rstd_col[:, 8:12], stat_bank[:], col_bank[:, 0:4], KV_LORA)
                tile.n += 16 + 16
                start_tile_2, start_group_2 = tile.n, 16

                def mla_split(g):
                    if g % 2:
                        act.wait_ge(o_taken, start_group_2 + g + 1)
                        if g // 2 >= 2:
                            act.wait_ge(tile_full, start_tile_2 + 8 * (g // 2 - 1))
                        hi_g(g // 2, from_t=False)
                attention("mla", UNITS, n_group=mla_split)
                tile.n += 24
                back(True, "mlp1" if stop > 6 else None)
            if stop > 6:
                mlp(None)
            if stop != 3:
                root(rstd[:, 0, :], None, stat_bank[:], None, D)


def kernel(**inputs):
    import concourse.bacc as bacc
    from concourse.bass_utils import run_bass_kernel_spmd

    nc = bacc.Bacc("TRN2", target_bir_lowering=False, num_devices=1)
    a = {n: np.asarray(v) for n, v in inputs.items()}
    arrays = {}

    def give(name, v):
        arrays[name] = np.ascontiguousarray(v)

    for name in ("x", "mem", "attn_norm_g", "w_in", "b_forget", "fox_out_g", "sb_out_g", "w_out", "xattn_norm_g",
                 "mem_norm_g", "w_mq", "w_mkv", "w_mo", "ffn_norm_g", "w_up", "conv_b", "w_down", "positions_2",
                 "a_w_in_2", "a_ln_v_g_2", "a_ln_v_b_2", "a_w_s_2", "a_w_out_2", "b_w_q_a_2",
                 "b_q_norm_g_2", "b_w_q_b_2", "b_w_o_2"):
        give(name, a[name][0])
    for name in ("final_norm_g", "kv_src_norm_g_2", "kv_w_a_2", "kv_a_norm_g_2", "kv_w_b_2", "final_norm_g_2"):
        give(name, a[name])
    give("a_b_s_2", a["a_b_s_2"][0])
    for i in range(3):
        give(f"conv_w{i}", a["conv_w"][0, i])
    for i in range(2):
        give(f"mix{i}", a["norm_mix_g_2"][i])
        give(f"mlp{i}", a["norm_mlp_g_2"][i])
        give(f"w1_{i}", a["mlp_w1_2"][i])
        give(f"w2_{i}", a["mlp_w2_2"][i])
    w = {n: nc.dram_tensor(n, v.shape, mybir.dt.from_np(v.dtype), kind="ExternalInput").ap()
         for n, v in arrays.items()}
    out = nc.dram_tensor("out", (1, S, D), F32, kind="ExternalOutput").ap()
    build(nc, w, out[0])
    r = run_bass_kernel_spmd(nc, [arrays], core_ids=[0])
    return r.results[0]["out"]
```

```python
from contextlib import ExitStack, contextmanager

import numpy as np

import concourse.bass as bass
from concourse import mybir

F32 = mybir.dt.float32
F32R = mybir.dt.float32r
I32 = mybir.dt.int32
ALU = mybir.AluOpType
ACT = mybir.ActivationFunctionType
AX = mybir.AxisListType

P = 128
S = 512
D = 1024
KT = D // P
TT = S // P
NMEM = 256
MT = NMEM // P
HEADS = 8
HD = 64
MEM_HEADS = 4
D_FF = 2816
GATE = 2048
D_FF_2 = 4096
Q_LORA, KV_LORA = 384, 256
NOPE, ROPE, VH = 128, 64, 128
MLA_HEADS = 8
EPS = 1e-6
MASKED = -3.0e38
CONSTANTS = 14
SLOT = 2048
COLS = 256
GRAN = 256

VECTORS = [
    [("attn_norm_g", 8), ("fox_out_g", 4), ("sb_out_g", 4), ("xattn_norm_g", 8), ("mem_norm_g", 8),
     ("ffn_norm_g", 8), ("conv_w0", 44), ("conv_w1", 44)],
    [("conv_w2", 44), ("conv_b", 44), ("final_norm_g", 8), ("mix0", 8), ("mix1", 8), ("mlp0", 8), ("mlp1", 8)],
    [("a_ln_v_g_2", 16), ("a_ln_v_b_2", 16), ("b_q_norm_g_2", 3), ("kv_src_norm_g_2", 8),
     ("kv_a_norm_g_2", 2), ("final_norm_g_2", 8)],
]
COLUMN = {}
_at = 0
for _group in VECTORS:
    for _name, _rows in _group:
        COLUMN[_name] = _at
        _at += _rows
NVEC = _at


class Count:

    def __init__(self):
        self.n, self.reg, self.per = 0, None, 0

    def at(self, value):
        return value if self.reg is None else self.reg * self.per + value


@contextmanager
def loop(engine, times, counts):
    start = [c.n for c, _ in counts]
    with engine.Fori(0, times) as i:
        for c, per in counts:
            c.reg, c.per = i, per
        yield i
    for (c, per), n in zip(counts, start):
        assert c.n - n == per, (c.n - n, per)
        c.n, c.reg = n + per * times, None


def weight_stream(w):
    def columns(name, first, n=COLS, tiles=2, stride=0):
        v = w[name].rearrange("(k p) n -> p k n", p=P)
        def parts(raw, i):
            return [(raw.rearrange("p (k n) -> p k n", n=COLS)[:, :, 0:n], v[:, :, bass.ds(i * stride + first, n)])]
        return SLOT, tiles, parts, max(n, P)

    def rows(name, granule, stride=0):
        v = w[name].rearrange("(k p) n -> p k n", p=P)
        def parts(raw, i):
            return [(raw.rearrange("p (k n) -> p k n", k=2), v[:, bass.ds(i * stride + 2 * granule, 2), :])]
        return SLOT, KT, parts, 0

    def k_rope(raw, i):
        v = w["kv_w_a_2"].rearrange("(k p) n -> p k n", p=P)
        d = raw.rearrange("p (k n) -> p k n", n=COLS)
        a, b = v[:, :, KV_LORA:KV_LORA + 32], v[:, :, KV_LORA + 32:KV_LORA + 64]
        return [(d[:, :, 0:32], a), (d[:, :, 32:64], b), (d[:, :, 64:96], b), (d[:, :, 96:128], a)]

    def q_heads(pair):
        v = w["b_w_q_b_2"].rearrange("(k p) n -> p k n", p=P)
        def parts(raw, i):
            d = raw[:, 0:3 * 512].rearrange("p (k n) -> p k n", n=512)
            out = []
            for j in range(2):
                at = (2 * pair + j) * (NOPE + ROPE)
                out += [(d[:, :, 256 * j:256 * j + 192], v[:, :, at:at + 192]),
                        (d[:, :, 256 * j + 192:256 * j + 224], v[:, :, at + 160:at + 192]),
                        (d[:, :, 256 * j + 224:256 * j + 256], v[:, :, at + 128:at + 160])]
            return out
        return 3 * 512, 4, parts, 0

    def kv_heads(c):
        v = w["kv_w_b_2"].rearrange("(k p) n -> p k n", p=P)
        return SLOT, 8, lambda raw, i: [(raw.rearrange("p (k n) -> p k n", k=2), v[:, :, 1024 * c:1024 * c + 1024])], 0

    def mlp(up, down):
        u = lambda g, s=0: columns(up, COLS * g, stride=s)
        d = lambda g, s=0: rows(down, g, stride=s)
        return [u(0), u(1), ("loop", 7, [d(0, 4), u(2, 512), d(1, 4), u(3, 512)]), d(14), d(15)]

    g = lambda n, s=0: columns("w_up", COLS * n, stride=s)
    v = lambda n, s=0: columns("w_up", D_FF + COLS * n, stride=s)
    d = lambda n, s=0: rows("w_down", n, stride=s)
    w_in = lambda kind, n=2: [columns("w_in", HEADS * HD * kind + COLS * c) for c in range(n)]
    mkv = lambda *cs: [columns("w_mkv", COLS * c, tiles=2 if c < 4 else 1) for c in cs]
    out = [("tiles", KT)] + w_in(0) + [("tiles", KT), columns("w_in", 6 * HEADS * HD, n=HEADS, tiles=1)]
    out += w_in(1) + w_in(2) + mkv(0, 1, 2, 3) + w_in(3) + w_in(4) + w_in(5) + mkv(4, 5, 6)
    out += [rows("w_out", c) for c in range(2)] + mkv(7) + [rows("w_out", c) for c in range(2, 4)]
    out += [columns("w_mq", COLS * c) for c in range(4)] + [rows("w_mo", c) for c in range(4)]
    out += [g(0), v(0), g(1), v(1), ("loop", 4, [d(0, 4), g(2, 512), v(2, 512), d(1, 4), g(3, 512), v(3, 512)]),
            d(8), g(10), v(10), d(9), d(10)]
    gate_v, gate_u = ([columns("a_w_in_2", at + COLS * c) for c in range(8)] for at in (GATE, 0))
    out += gate_v[0:6] + [("tiles", 2)] + gate_v[6:8] + [("tiles", 2)]
    out += gate_u[0:7] + [("tiles", 2)] + gate_u[7:8]
    for c in range(8):
        out += [("tiles", 2)] * (c < 7) + [rows("a_w_out_2", c)]
    out += mlp("w1_0", "w2_0")
    out += [columns("b_w_q_a_2", 0), columns("b_w_q_a_2", 256, n=128, tiles=1)]
    out += [columns("kv_w_a_2", 0), (SLOT, 1, k_rope, P)]
    out += [q_heads(p) for p in range(4)] + [kv_heads(c) for c in range(2)]
    out += [rows("b_w_o_2", c) for c in range(4)]
    out += mlp("w1_1", "w2_1")
    return out


def build(nc, w, out):
    x_in, mem_in = w["x"], w["mem"]
    freq = nc.inline_tensor(np.tile((np.float32(10000.0) ** (-np.arange(0, ROPE, 2, dtype=np.float32)
                                    / np.float32(ROPE))).astype(np.float32), 4).reshape(P, 1), name="inv_freq")

    with ExitStack() as ctx:
        def sb(name, shape, dt=F32):
            return ctx.enter_context(nc.sbuf_tensor(name, shape, dt))

        def sem(name):
            return ctx.enter_context(nc.semaphore(name))

        raw = sb("raw", [P, 2, SLOT])
        w_hi = sb("w_hi", [P, 2, SLOT], F32R)
        w_lo = sb("w_lo", [P, 2, SLOT], F32R)
        x = sb("resid", [P, KT, S])
        h_hi = sb("h_hi", [P, KT, S], F32R)
        h_lo = sb("h_lo", [P, KT, S], F32R)
        g_hi = sb("g_hi", [P, 4, S], F32R)
        g_lo = sb("g_lo", [P, 4, S], F32R)
        vec = sb("vec", [P, NVEC])
        ident = sb("ident", [P, P])
        ones = sb("ones", [P, P])
        causal = sb("causal", [P, P])
        strict = sb("strict", [P, P])
        chunked = sb("chunked", [P, P])
        rstd = sb("rstd", [P, 2, S])
        neg_c = sb("neg_c", [P, S], F32R)
        pick = sb("pick", [P, HEADS], F32R)
        rstd_col = sb("rstd_col", [P, 12])
        small = sb("small", [P, 48])
        biases = sb("biases", [P, 2, P])
        arena = sb("arena", [P, 21504])

        def at(start, *shape):
            n = int(np.prod(shape))
            v = arena[:, start:start + n]
            if len(shape) == 2:
                return v.rearrange("p (a b) -> p a b", b=shape[1])
            return v

        x_stage, mem_stage = at(0, TT, D), at(14336, MT, D)
        vec_stage = at(12288, 3, P)
        mem_t = at(19456, KT, NMEM)
        sq_mem, sq_x = at(16384, KT, NMEM), at(8192, KT, S)
        sq, sq_normed = at(0, KT, S), at(4096, KT, S)
        sq_fox = at(18432, 4, S)
        fox_q, fox_k, fox_v, mix_o = at(0, 8, S), at(4096, 4, S), at(6144, TT, S), at(8192, KT, S)
        sq_sb = mix_o[:, 0:4, :]
        mem_k, mem_v = at(12288, KT, NMEM), at(14336, MT, D)
        mem_q = at(0, KT, S)
        prob, prob_t, keep = at(16384, 2, S), at(17408, 2, S), at(18432, 2, S)
        t_buf, r_buf = at(19456, 2, S), at(20480, 2, S)
        stick = at(20480, S + 1)
        f_z, f_a = at(12800, S), at(13312, S)
        rstd_fox, rstd_kv = at(19456, S), at(17408, S)
        conv_u, conv_y, conv_s = at(4096, 4, S + 2), at(6656, 4, S), at(8704, 2, S)
        gm_v, gm_u = at(0, TT, GATE), at(8192, 16, S)
        bs_all, ws_t, ws_sum, ws_stage = at(16384, 8, P), at(17408, 8, P), at(18432, 8, P), at(8192, 8, P)
        lat_q, lat_kv, lat_sq = at(0, 3, S), at(1536, 2, S), at(4096, 5, S)
        mla_q, mla_k, mla_v, mla_qr = at(0, 8, S), at(4096, 8, S), at(8192, TT, 1024), at(12288, 8, S)
        rope_k, rope_t = at(18432, S), at(18944, S)
        ang, turns, pos_i = at(20480, S), at(20992, S), at(6656, S)
        rope_a, rope_b = at(20480, S), at(20992, S)
        y_final, out_stage = at(4096, KT, S), at(8192, TT, D)
        OUT_PIECES = [(half, t) for half in range(2) for t in range(TT)]
        neg_max, row_sum, row_inv = small[:, 0:2], small[:, 2:4], small[:, 4:6]
        eps_t, invf, phase = small[:, 6:7], small[:, 7:8], small[:, 8:9]
        one_col, b_forget = small[:, 9:10], small[:, 10:11]
        mix0_gain = small[:, 24:32]
        ln_mv, ln_std = small[:, 12:20].rearrange("p (t s) -> p t s", s=2), small[:, 20:24]
        ln_part = biases.rearrange("p a b -> p (a b)")[:, 0:24].rearrange("p (c s) -> p c s", s=6)

        bank = [ctx.enter_context(nc.psum_tensor(f"bank{i}", [P, S], F32)) for i in range(8)]
        tile_bank, s_bank, pt_bank, o_bank = bank[0:4], bank[4:6], bank[6], bank[7]
        col_bank, stat_bank = pt_bank, o_bank

        vec_loaded = sem("vec_loaded")
        mem_loaded = sem("mem_loaded")
        x_loaded = [sem(f"x_loaded{c}") for c in range(4)]
        f_loaded = sem("f_loaded")
        gm_loaded = sem("gm_loaded")
        pos_loaded = sem("pos_loaded")
        consts = sem("consts")
        w_loaded = [sem("w_loaded0"), sem("w_loaded1")]
        w_hi_done = sem("w_hi_done")
        w_split = sem("w_split")
        pool_gate = sem("pool_gate")
        act_gate = sem("act_gate")
        tile_full = sem("tile_full")
        tile_taken = sem("tile_taken")
        vec_t = sem("vec_t")
        hi_done = sem("hi_done")
        h_ready = sem("h_ready")
        g_ready = sem("g_ready")
        sq_done = sem("sq_done")
        acc_ready = sem("acc_ready")
        stat_full = sem("stat_full")
        std_done = sem("std_done")
        own = sem("own")
        act_own = sem("act_own")
        act_out = sem("act_out")
        t_made = sem("t_made")
        s_full = sem("s_full")
        s_masked = sem("s_masked")
        s_taken = sem("s_taken")
        p_ready = sem("p_ready")
        pt_full = sem("pt_full")
        pt_taken = sem("pt_taken")
        pv_done = sem("pv_done")
        o_taken = sem("o_taken")
        c_ready = sem("c_ready")
        gm_ready = sem("gm_ready")
        y_ready = sem("y_ready")
        out_full = sem("out_full")
        out_vector = sem("out_vector")
        out_scalar = sem("out_scalar")
        stored = sem("stored")

        def cols_view(t, slot):
            return t[:, slot, :].rearrange("p (k n) -> p k n", n=COLS)

        def rows_view(t, slot):
            return t[:, slot, :].rearrange("p (k n) -> p k n", k=2)

        def gain(name, i=0):
            c = COLUMN[name] + i
            return vec[:, bass.ds(c, 1)]

        def out_banks(tiles):
            four = [tile_bank[(tiles + q) % 4] for q in range(4)]
            return four + [s_bank[0], s_bank[1], o_bank, four[0]]

        UNITS = [(h, i) for h in range(8) for i in range(TT)]
        BACK_STEPS = range(15, 35, 2)
        MEM_UNITS = [(h, i) for h in range(MEM_HEADS) for i in range(TT)]
        GROUP = {"fox": 2 * TT, "sb": 2 * TT, "mem": 2, "mla": TT}

        def keys(kind, i):
            return NMEM if kind == "mem" else P * (i + 1)

        stream = weight_stream(w)
        block = ctx.enter_context(nc.Block())

        @block.sync
        def _(sp):
            chunk = Count()
            x_cols = x_in.rearrange("(t p) n -> p t n", p=P)

            def load(item, i):
                _, _, parts, _ = item
                slot = chunk.n % 2
                if chunk.n == 1:
                    for c in range(4):
                        sp.dma_start(x_stage[:, :, 256 * c:256 * c + 256], x_cols[:, :, 256 * c:256 * c + 256])\
                          .then_inc(x_loaded[c], 16)
                if chunk.n == 2:
                    sp.dma_start(mem_stage, mem_in.rearrange("(t p) n -> p t n", p=P)).then_inc(mem_loaded, 16)
                if chunk.n >= 2:
                    sp.wait_ge(w_split, chunk.at(chunk.n - 1))
                for dst, src in parts(raw[:, slot, :], i):
                    sp.dma_start(dst, src).then_inc(w_loaded[slot], 16)
                chunk.n += 1

            for item in stream:
                if item[0] == "tiles":
                    continue
                if item[0] == "loop":
                    with loop(sp, item[1], [(chunk, len(item[2]))]) as i:
                        for part in item[2]:
                            load(part, i)
                else:
                    load(item, 0)
            for k in range(4):
                half, t = OUT_PIECES[2 * k]
                sp.wait_ge(out_vector, k + 1)
                sp.wait_ge(out_scalar, k + 1)
                cut = slice(512 * half, 512 * half + 512)
                sp.dma_start(out.rearrange("(t p) n -> p t n", p=P)[:, t:t + 2, cut], out_stage[:, t:t + 2, cut])\
                  .then_inc(stored, 16)
            sp.wait_ge(stored, 16 * 4)

        @block.gpsimd
        def _(pool):
            def in_turn(n, ins):
                ins.then_inc(consts, 1)
                pool.wait_ge(consts, n)

            G = nc.gpsimd
            in_turn(1, G.memset(ident[:], 0.0))
            in_turn(2, G.memset(ones[:], 1.0))
            in_turn(3, G.memset(causal[:], 0.0))
            in_turn(4, G.memset(strict[:], 0.0))
            in_turn(5, G.memset(chunked[:], 0.0))
            in_turn(6, G.memset(eps_t, EPS))
            in_turn(7, G.memset(one_col, 1.0))
            in_turn(8, G.memset(phase[0:64], float(np.pi / 2)))
            in_turn(9, G.memset(phase[64:96], float(np.pi)))
            in_turn(10, G.memset(phase[96:128], 0.0))
            in_turn(11, G.memset(chunked[0:64, 64:128], MASKED))
            in_turn(12, G.affine_select(out=ident[:], in_=ident[:], compare_op=ALU.not_equal, fill=1.0, base=0,
                                        pattern=[[-1, P]], channel_multiplier=1))
            in_turn(13, G.affine_select(out=causal[:], in_=causal[:], compare_op=ALU.is_ge, fill=MASKED, base=0,
                                        pattern=[[-1, P]], channel_multiplier=1))
            in_turn(CONSTANTS, G.affine_select(out=strict[:], in_=strict[:], compare_op=ALU.is_gt, fill=MASKED, base=0,
                                               pattern=[[-1, P]], channel_multiplier=1))
            chunk, tile, loads = Count(), Count(), [Count(), Count()]
            ends = [0, 0]

            def split(item):
                size, tiles, parts, used = item
                slot = chunk.n % 2
                loads[slot].n += len(parts(raw[:, slot, :], 0))
                pool.wait_ge(w_loaded[slot], loads[slot].at(loads[slot].n) * 16)
                if chunk.n >= 2:
                    pool.wait_ge(tile_full, tile.at(ends[0]))
                pool.sem_inc(pool_gate, 1)
                hi, lo, src = w_hi[:, slot, 0:size], w_lo[:, slot, 0:size], raw[:, slot, 0:size]
                one = one_col.to_broadcast([P, size])
                if 0 < used < COLS:
                    hi, lo, src = (t.rearrange("p (k n) -> p k n", n=COLS)[:, :, 0:used] for t in (hi, lo, src))
                    one = one_col.unsqueeze(2).to_broadcast([P, KT, used])
                nc.gpsimd.tensor_tensor(hi, src, one, ALU.mult).then_inc(w_hi_done, 1)
                chunk.n += 1
                pool.wait_ge(w_hi_done, chunk.at(chunk.n))
                nc.gpsimd.tensor_tensor(lo, src, hi.bitcast(F32), ALU.subtract).then_inc(w_split, 1)
                tile.n += tiles
                ends[:] = [ends[1], tile.n]

            for item in stream:
                if item[0] == "tiles":
                    tile.n += item[1]
                elif item[0] == "loop":
                    each, tiles, entry = len(item[2]), sum(c[1] for c in item[2]), list(ends)
                    with loop(pool, item[1], [(chunk, each), (tile, tiles),
                                              (loads[0], each // 2), (loads[1], each // 2)]):
                        for part in item[2]:
                            split(part)
                    assert ends == [e + tiles for e in entry]
                    ends[:] = [e + tiles * item[1] for e in entry]
                else:
                    split(item)

        @block.tensor
        def _(pe):
            chunk, tile, h_n, g_n, stats = Count(), Count(), Count(), Count(), Count()
            unit, group = Count(), Count()

            def wait_chunk():
                pe.wait_ge(w_split, chunk.at(chunk.n + 1))

            def next_bank():
                if tile.n >= 4:
                    pe.wait_ge(tile_taken, tile.at(tile.n - 3))
                return tile_bank[tile.n % 4]

            def full(last):
                last.then_inc(tile_full, 1)
                tile.n += 1

            def split_sum(dst, stationary, moving, arrive=None, part=None):
                n = len(stationary)
                for k in part or range(n):
                    (a_hi, a_lo), (b_hi, b_lo) = stationary[k], moving[k]
                    if arrive is not None:
                        pe.wait_ge(h_ready, arrive + k + 1)
                    nc.tensor.matmul(dst, a_hi, b_hi, start=(k == 0), stop=False)
                    nc.tensor.matmul(dst, a_hi, b_lo, start=False, stop=False)
                    last = nc.tensor.matmul(dst, a_lo, b_hi, start=False, stop=(k == n - 1))
                return last

            def h_tiles(n=KT, first=0, cut=slice(0, S)):
                return [(h_hi[:, first + k, cut], h_lo[:, first + k, cut]) for k in range(n)]

            def mem_tiles(cut=slice(0, NMEM)):
                views = [t[:].rearrange("p a b -> p (a b)").rearrange("p (k n) -> p k n", n=NMEM) for t in (g_hi, g_lo)]
                return [(views[0][:, k, cut], views[1][:, k, cut]) for k in range(KT)]

            def w_tiles(n, cut, view=cols_view):
                slot = chunk.n % 2
                return [(view(w_hi, slot)[:, k, cut], view(w_lo, slot)[:, k, cut]) for k in range(n)]

            def by_feature(tiles=2, moving=None, arrive=None, n_tokens=S):
                wait_chunk()
                for j in range(tiles):
                    dst = next_bank()[:, 0:n_tokens]
                    full(split_sum(dst, w_tiles(KT, slice(P * j, P * j + P)), moving or h_tiles(),
                                   arrive if j == 0 else None))
                chunk.n += 1

            def by_token(pairs=2, stationary=h_tiles, arrive=None):
                wait_chunk()
                for j in range(pairs):
                    b = next_bank()
                    for half in range(2):
                        t = 2 * j + half
                        last = split_sum(b[:, COLS * half:COLS * half + COLS], stationary(cut=slice(P * t, P * t + P)),
                                         w_tiles(KT, slice(0, COLS)), arrive if t == 0 else None)
                    full(last)
                chunk.n += 1

            def back(granule, tiles=range(KT), in_h=False):
                p = granule % 2
                if tiles[0] == 0:
                    wait_chunk()
                    if in_h:
                        pe.wait_ge(h_ready, h_n.n + 2)
                        h_n.n += 2
                    else:
                        pe.wait_ge(g_ready, g_n.at(g_n.n + 2))
                        g_n.n += 2
                moving = h_tiles(2, 2 * granule) if in_h else \
                    [(g_hi[:, 2 * p + k, :], g_lo[:, 2 * p + k, :]) for k in range(2)]
                for n in tiles:
                    dst = next_bank()
                    full(split_sum(dst[:], w_tiles(2, slice(P * n, P * n + P), rows_view), moving))
                if tiles[-1] == KT - 1:
                    chunk.n += 1

            def stat(acc, tokens=S, by_col=False, bank=stat_bank, col_at=0):
                pe.wait_ge(acc_ready, stats.n + 1)
                if group.n:
                    pe.wait_ge(o_taken, group.n)
                if stats.n:
                    pe.wait_ge(std_done, stats.n)
                if bank is not None:
                    last = nc.tensor.matmul(bank[:, 0:tokens], ones[:], acc, start=True, stop=True)
                for t in range(tokens // P if by_col else 0):
                    last = nc.tensor.matmul(col_bank[:, col_at + t:col_at + t + 1], acc[:, P * t:P * t + P], ones[:, 0:1],
                                            start=True, stop=True)
                last.then_inc(stat_full, 1)
                stats.n += 1

            def turn(src, n_tok_tiles, tokens, loaded):
                for n in range(KT):
                    if n % (KT // len(loaded)) == 0:
                        pe.wait_ge(loaded[n * len(loaded) // KT], 16)
                    b = next_bank()
                    for t in range(n_tok_tiles):
                        last = nc.tensor.transpose(b[:, P * t:P * t + P], src[:, t, P * n:P * n + P], ident[:])
                    full(last)

            def attention(kind, units, scores, values, n_after=lambda s: None, v_tiles=0):
                n = len(units)
                per = GROUP[kind]
                first, first_group = unit.n, group.n
                pe.wait_ge(tile_taken, tile.n - v_tiles)
                v_end = tile.n
                for s in range(n + 3):
                    if s < n:
                        u = first + s
                        if u >= 2:
                            pe.wait_ge(s_taken, u - 1)
                        h, i = units[s]
                        scores(h, i, s_bank[u % 2][:, 0:keys(kind, i)]).then_inc(s_full, 1)
                    if 0 <= s - 3 < n:
                        u = first + s - 3
                        h, i = units[s - 3]
                        pe.wait_ge(pt_taken, u + 1)
                        if s == 3:
                            pe.wait_ge(tile_taken, v_end)
                        if (s - 3) % per == 0:
                            pe.wait_ge(o_taken, first_group + (s - 3) // per)
                        values(h, i, prob_t[:, u % 2, :]).then_inc(pv_done, 1)
                        if (s - 3) % per == per - 1:
                            group.n += 1
                    if 0 <= s - 2 < n:
                        u = first + s - 2
                        h, i = units[s - 2]
                        pe.wait_ge(p_ready, u + 1)
                        if u >= 1:
                            pe.wait_ge(pt_taken, u)
                        for k in range(keys(kind, i) // P):
                            last = nc.tensor.transpose(pt_bank[:, P * k:P * k + P],
                                                       prob[:, u % 2, P * k:P * k + P], ident[:])
                        last.then_inc(pt_full, 1)
                    n_after(s)
                unit.n += n

            def several(ops):
                for j, (dst, a, b, first, last) in enumerate(ops):
                    ins = nc.tensor.matmul(dst, a, b, start=first, stop=last)
                return ins

            pe.wait_ge(consts, CONSTANTS)
            pe.wait_ge(vec_loaded, 16)
            for g, rows in enumerate(VECTORS):
                n = sum(r for _, r in rows)
                last = nc.tensor.transpose(s_bank[0][:, P * g:P * g + n], vec_stage[0:n, g, :], ident[0:n, 0:n])
            last.then_inc(vec_t, 1)

            turn(x_stage, TT, S, x_loaded)

            def mem_keys(s):
                j, quarter = s % 8 // 4, s % 4
                if s % 8 == 0:
                    wait_chunk()
                dst = next_bank()[:, 0:NMEM] if quarter == 0 else tile_bank[tile.n % 4][:, 0:NMEM]
                last = split_sum(dst, w_tiles(KT, slice(P * j, P * j + P)), mem_tiles(),
                                 part=range(2 * quarter, 2 * quarter + 2))
                if quarter == 3:
                    full(last)
                if s % 8 == 7:
                    chunk.n += 1

            def mem_values_of(s):
                t, half = s % 4 // 2, s % 2
                if s % 4 == 0:
                    wait_chunk()
                b = next_bank() if s % 4 == 0 else tile_bank[tile.n % 4]
                last = split_sum(b[:, COLS * t:COLS * t + COLS], mem_tiles(slice(P * t, P * t + P)),
                                 w_tiles(KT, slice(0, COLS)), part=range(4 * half, 4 * half + 4))
                if s % 4 == 3:
                    full(last)
                    chunk.n += 1

            def fox_scores(h, i, dst):
                q = fox_q[:, h, P * i:P * i + P]
                n = P * (i + 1)
                return several([(dst, q, fox_k[:, h // 2, 0:n], True, False),
                                (dst, pick[:, h:h + 1].to_broadcast([P, P]), neg_c[:, 0:n], False, True)])

            def sb_scores(h, i, dst):
                return several([(dst, fox_q[:, h, P * i:P * i + P], fox_k[:, h // 2, 0:P * (i + 1)], True, True)])

            def head_values(h, i, pt):
                r = HD * (h % 2)
                return several([(o_bank[r:r + HD, P * i:P * i + P], fox_v[:, k, HD * h:HD * h + HD],
                                 pt[:, P * k:P * k + P], k == 0, k == i) for k in range(i + 1)])

            by_feature(arrive=h_n.n)
            h_n.n += KT
            stat(sq_x[:, 0, :], by_col=True)
            by_feature()
            turn(mem_stage, MT, NMEM, [mem_loaded])
            by_feature(1)
            by_feature()
            by_feature()
            stat(sq_mem[:, 0, :], NMEM, by_col=True)
            by_token()
            by_token()
            pe.wait_ge(h_ready, h_n.n + KT)
            h_n.n += KT
            pe.wait_ge(c_ready, 1)
            attention("fox", UNITS, fox_scores, head_values, lambda s: mem_keys(s - 3) if s >= 3 else None,
                      v_tiles=4)
            by_feature()
            stat(sq_fox[:, 0, :])
            for c in range(3):
                by_feature()
            by_token()
            by_token()

            def beside_sb(s):
                if 3 <= s < 15:
                    mem_values_of(s - 3)
                elif s in BACK_STEPS:
                    n = BACK_STEPS.index(s)
                    back(n // KT, [n % KT], in_h=True)

            attention("sb", UNITS, sb_scores, head_values, beside_sb, v_tiles=4)

            back(1, range(2, 6), in_h=True)
            stat(sq_sb[:, 0, :])
            back(1, range(6, KT), in_h=True)
            for piece in range(4):
                mem_values_of(piece)
            back(2, in_h=True)
            back(3)
            by_feature(arrive=h_n.n)
            h_n.n += KT
            stat(sq[:, 0, :])
            for c in range(3):
                by_feature()

            def mem_scores(h, i, dst):
                return several([(dst, mem_q[:, 2 * h + k, P * i:P * i + P], mem_k[:, 2 * h + k, :], k == 0, k == 1)
                                for k in range(2)])

            def mem_values(h, i, pt):
                return several([(o_bank[:, 256 * j + P * (i % 2):256 * j + P * (i % 2) + P],
                                 mem_v[:, k, 256 * h + P * j:256 * h + P * j + P], pt[:, P * k:P * k + P],
                                 k == 0, k == 1) for j in range(2) for k in range(2)])

            attention("mem", MEM_UNITS, mem_scores, mem_values,
                      lambda s: back((s - 8) // 4, [s % 4 * 2, s % 4 * 2 + 1]) if s >= 8 else None)
            back(2, [6, 7])
            back(3)
            by_feature(arrive=h_n.n)
            h_n.n += KT
            stat(sq[:, 0, :])
            by_feature()
            for c in range(2):
                by_feature()
            per = [(chunk, 6), (tile, 24), (g_n, 4)]
            with loop(pe, 4, per):
                for g in range(2):
                    back(g)
                    by_feature()
                    by_feature()
            back(8)
            by_feature()
            by_feature()
            back(9)
            back(10)
            by_token(arrive=h_n.n)
            h_n.n += KT
            stat(sq[:, 0, :], by_col=True)
            stat(sq_normed[:, 0, :], by_col=True, bank=s_bank[0], col_at=TT)
            by_token()
            with loop(pe, 2, [(chunk, 2), (tile, 4)]):
                by_token()
                by_token()
            pe.wait_ge(gm_loaded, 16 * 2)
            for half in range(2):
                b = next_bank()
                for g in range(4):
                    last = nc.tensor.transpose(b[:, P * g:P * g + P], ws_stage[:, 4 * half + g, :], ident[:])
                full(last)
            by_token()
            by_token()
            for half in range(2):
                b = next_bank()
                if half == 0:
                    pe.wait_ge(gm_ready, 1)
                full(nc.tensor.matmul(b[:], ones[:], ws_t[:, 4 * half:4 * half + 4, :], start=True, stop=True))
            with loop(pe, 3, [(chunk, 2), (tile, 4)]):
                by_feature()
                by_feature()
            by_feature()

            def spatial(g):
                for j in range(2):
                    b = next_bank()
                    for t in range(TT):
                        c = 256 * g + P * j
                        last = nc.tensor.matmul(b[:, P * t:P * t + P], gm_v[:, t, c:c + P], ws_t[:, g, :],
                                                start=True, stop=True)
                    full(last)

            pe.wait_ge(gm_ready, 2)
            spatial(0)
            by_feature()
            for g in range(1, 8):
                spatial(g)
                back(g - 1)
            back(7)

            def mlp():
                by_feature(arrive=h_n.n)
                h_n.n += KT
                stat(sq[:, 0, :])
                by_feature()
                with loop(pe, 7, [(chunk, 4), (tile, 20), (g_n, 4)]):
                    for g in range(2):
                        back(g)
                        by_feature()
                back(14)
                back(15)

            mlp()
            by_feature(arrive=h_n.n)
            h_n.n += KT
            stat(sq[:, 0, :])
            by_feature(1)
            kv_source = [(g_hi[:, k, :], g_lo[:, k, :]) for k in range(4)] + h_tiles(4, 4)
            by_feature(moving=kv_source, arrive=h_n.n)
            by_feature(1, moving=kv_source)
            h_n.n += KT
            stat(lat_sq[:, 0, :])
            pe.wait_ge(h_ready, h_n.n + 3)
            h_n.n += 3
            for p in range(4):
                wait_chunk()
                slot = chunk.n % 2
                views = [t[:, slot, 0:1536].rearrange("p (k n) -> p k n", n=512) for t in (w_hi, w_lo)]
                for j in range(4):
                    dst = next_bank()
                    full(split_sum(dst[:], [(views[0][:, k, P * j:P * j + P], views[1][:, k, P * j:P * j + P])
                                            for k in range(3)], h_tiles(3)))
                chunk.n += 1
                if p == 1:
                    stat(lat_sq[:, 3, :], by_col=True)
            pe.wait_ge(h_ready, h_n.n + 2)
            h_n.n += 2
            for c in range(2):
                wait_chunk()
                for h in range(4):
                    dst = next_bank()
                    full(split_sum(dst[:], w_tiles(2, slice(256 * h, 256 * h + P), rows_view), h_tiles(2, 3)))
                slot = chunk.n % 2
                vals = [tuple(rows_view(t, slot)[:, k, :].rearrange("p (h n) -> p h n", n=256)[:, :, P:256]
                              for t in (w_hi, w_lo)) for k in range(2)]
                for t in range(TT):
                    dst = next_bank()
                    full(split_sum(dst[:].rearrange("p (h n) -> p h n", n=P),
                                   h_tiles(2, 3, slice(P * t, P * t + P)), vals))
                chunk.n += 1

            def mla_scores(h, i, dst):
                n = P * (i + 1)
                return several([(dst, mla_q[:, h, P * i:P * i + P], mla_k[:, h, 0:n], True, False),
                                (dst, mla_qr[:, h, P * i:P * i + P], rope_k[:, 0:n], False, True)])

            def mla_values(h, i, pt):
                return several([(o_bank[:, P * i:P * i + P], mla_v[:, k, P * h:P * h + P],
                                 pt[:, P * k:P * k + P], k == 0, k == i) for k in range(i + 1)])

            attention("mla", UNITS, mla_scores, mla_values,
                      lambda s: back((s - 12) // 8, [(s - 12) % 8]) if s >= 12 else None, v_tiles=4)
            back(2, [7])
            back(3)
            mlp()
            for q, (half, t) in enumerate(OUT_PIECES):
                if t == 0:
                    pe.wait_ge(y_ready, 4 * half + 4)
                if q < 4:
                    pe.wait_ge(tile_taken, tile.n - 3 + q)
                elif q == 4:
                    stat(sq[:, 0, :], by_col=True, bank=None)
                elif q == 7:
                    pe.wait_ge(out_vector, 1)
                for n in range(4):
                    last = nc.tensor.transpose(out_banks(tile.n)[q][:, P * n:P * n + P],
                                               y_final[:, 4 * half + n, P * t:P * t + P], ident[:])
                last.then_inc(out_full, 1)

        @block.vector
        def _(dve):
            V = nc.vector
            tile, hi_n, g_n, mine, stats, acts, made = (Count() for _ in range(7))
            sq_n, unit, group = Count(), Count(), Count()

            def keep_order(ins):
                ins.then_inc(own, 1)
                mine.n += 1

            def settle():
                dve.wait_ge(own, mine.at(mine.n))

            def take(fn):
                dve.wait_ge(tile_full, tile.at(tile.n + 1))
                b = tile_bank[tile.n % 4]
                fn(b).then_inc(tile_taken, 1)
                tile.n += 1

            def low_half(lo, hi, src, scale, ready):
                dve.wait_ge(hi_done, hi_n.at(hi_n.n + 1))
                hi_n.n += 1
                if scale is None:
                    V.tensor_tensor(lo, src, hi.bitcast(F32), ALU.subtract).then_inc(ready, 1)
                else:
                    V.scalar_tensor_tensor(lo, src, scale, hi.bitcast(F32), ALU.mult, ALU.subtract).then_inc(ready, 1)

            def lo_h(n, name):
                g = mix0_gain[:, n:n + 1] if name == "final, mix0" else gain(name, n)
                low_half(h_lo[:, n, :], h_hi[:, n, :], x[:, n, :], g, h_ready)

            def lo_g(granule, j, src):
                p = 2 * (granule % 2) + j
                low_half(g_lo[:, p, :], g_hi[:, p, :], src, None, g_ready)
                g_n.n += 1

            def lows_done():
                if g_n.n:
                    dve.wait_ge(g_ready, g_n.at(g_n.n))

            def sum_squares(s, n_tiles):
                sq_n.n += n_tiles
                dve.wait_ge(sq_done, sq_n.n)
                n = n_tiles
                while n > 1:
                    m = n // 2
                    ins = V.tensor_tensor(s[:, 0:m, :], s[:, 0:m, :], s[:, n - m:n, :], ALU.add)
                    n -= m
                    if n > 1:
                        keep_order(ins)
                        settle()
                ins.then_inc(acc_ready, 1)

            def finish_rstd(row, col=None):
                stats.n += 1
                dve.wait_ge(std_done, stats.n)
                ins = V.reciprocal(row, row)
                if col is not None:
                    keep_order(ins)
                    ins = V.reciprocal(col, col)
                keep_order(ins)
                settle()

            def back_tile(n):
                take(lambda b: V.tensor_tensor(x[:, n, :], b[:], x[:, n, :], ALU.add))

            def back(last=None):
                for n in range(KT):
                    back_tile(n)
                    if last and n >= 1:
                        lo_h(n - 1, last)
                if last:
                    lo_h(KT - 1, last)

            def scaled(dst, by, factor=None):
                def fn(b):
                    if factor is None:
                        return V.tensor_tensor(dst, b[:], by, ALU.mult)
                    return V.scalar_tensor_tensor(dst, b[:], factor, by, ALU.mult, ALU.mult)
                return fn

            def attention(kind, units, mask, out_group, between):
                n, per = len(units), GROUP[kind]
                first = unit.n
                for s in range(n + 4):
                    if 0 <= s - 2 < n:
                        u = first + s - 2
                        h, i = units[s - 2]
                        nk = keys(kind, i)
                        dve.wait_ge(s_taken, u + 1)
                        if kind == "sb":
                            dve.wait_ge(p_ready, u)
                            k_rev = keep[:, u % 2, 0:nk][:, ::-1]
                            keep_order(V.tensor_tensor_scan(stick[:, S - nk:S][:, ::-1], k_rev, k_rev, 1.0,
                                                            ALU.mult, ALU.min))
                            settle()
                            V.tensor_tensor(prob[:, u % 2, 0:nk], prob[:, u % 2, 0:nk],
                                            stick[:, S - nk + 1:S + 1], ALU.mult).then_inc(p_ready, 1)
                        else:
                            keep_order(V.reciprocal(row_inv[:, u % 2:u % 2 + 1], row_sum[:, u % 2:u % 2 + 1]))
                            settle()
                            V.tensor_scalar(prob[:, u % 2, 0:nk], prob[:, u % 2, 0:nk],
                                            row_inv[:, u % 2:u % 2 + 1], None, ALU.mult).then_inc(p_ready, 1)
                    between(s)
                    if s < n:
                        u = first + s
                        h, i = units[s]
                        nk = keys(kind, i)
                        b = s_bank[u % 2]
                        dve.wait_ge(s_full, u + 1)
                        if mask is not None:
                            ins = V.tensor_tensor(b[:, nk - P:nk], b[:, nk - P:nk], mask[:], ALU.add)
                            if kind != "sb":
                                keep_order(ins)
                                settle()
                        if kind != "sb":
                            ins = V.tensor_reduce(neg_max[:, u % 2:u % 2 + 1], b[:, 0:nk], AX.X, ALU.max, negate=True)
                        ins.then_inc(s_masked, 1)
                    if 0 <= s - 3 < n and (s - 3) % per == per - 1:
                        dve.wait_ge(pv_done, first + s - 3 + 1)
                        out_group((s - 3) // per, o_bank)
                        group.n += 1
                unit.n += n

            dve.wait_ge(vec_t, 1)
            keep_order(V.tensor_copy(vec[:], s_bank[0][:, 0:NVEC]))
            settle()
            for n in range(KT):
                take(lambda b: V.tensor_copy(x[:, n, :], b[:]))
                if n:
                    lo_h(n - 1, "attn_norm_g")
            lo_h(KT - 1, "attn_norm_g")
            V.tensor_tensor(pick[:], ident[:, 0:HEADS], ident[:, 32:32 + HEADS], ALU.add)
            for t in range(TT):
                keep_order(V.tensor_scalar(neg_c[:, P * t:P * t + P], ident[:], 0.0, None, ALU.mult))
            sum_squares(sq_x, KT)

            def mem_keys(n):
                take(lambda b: V.tensor_tensor(mem_k[:, n, :], b[:, 0:NMEM], rstd[:, 1, 0:NMEM], ALU.mult))

            def mem_values_of(c):
                def two_tokens(b):
                    for t in range(MT):
                        last = V.tensor_scalar(mem_v[:, t, COLS * c:COLS * c + COLS], b[:, COLS * t:COLS * t + COLS],
                                               rstd_col[:, 4 + t:5 + t], None, ALU.mult)
                    return last
                take(two_tokens)

            def head_queries():
                for n in range(4):
                    def two_heads(b):
                        for j in range(2):
                            r = slice(HD * j, HD * j + HD)
                            last = V.scalar_tensor_tensor(fox_q[r, 2 * n + j, :], b[r, :], HD ** -0.5, rstd[r, 0, :],
                                                          ALU.mult, ALU.mult)
                        return last
                    take(two_heads)

            def head_keys():
                for n in range(4):
                    take(scaled(fox_k[:, n, :], rstd[:, 0, :]))

            def head_values():
                for c in range(2):
                    for j in range(2):
                        def two_tokens(b):
                            for half in range(2):
                                t = 2 * j + half
                                last = V.tensor_scalar(fox_v[:, t, COLS * c:COLS * c + COLS],
                                                       b[:, COLS * half:COLS * half + COLS], rstd_col[:, t:t + 1],
                                                       None, ALU.mult)
                            return last
                        take(two_tokens)

            finish_rstd(rstd[:, 0, :], rstd_col[:, 0:4])
            for n in range(8):
                r = slice(HD, P) if n % 2 == 0 else slice(0, HD)
                V.memset(fox_q[r, n, :], 0.0)
            head_queries()
            for n in range(KT):
                take(lambda b: V.tensor_copy(mem_t[:, n, :], b[:, 0:NMEM]))
            take(lambda b: V.tensor_tensor(f_z[0:8, :], b[0:8, :], rstd[0:8, 0, :], ALU.mult))
            dve.wait_ge(tile_taken, tile.n)
            dve.wait_ge(f_loaded, 16)
            V.tensor_scalar(f_z[0:8, :], f_z[0:8, :], b_forget[0:8], None, ALU.add).then_inc(t_made, 1)
            made.n += 1
            m_hi, m_lo = (t[:].rearrange("p a b -> p (a b)").rearrange("p (k n) -> p k n", n=NMEM) for t in (g_hi, g_lo))
            for n in range(KT):
                low_half(m_lo[:, n, :], m_hi[:, n, :], mem_t[:, n, :], gain("mem_norm_g", n), h_ready)
            sum_squares(sq_mem, KT)
            acts.n += 1
            dve.wait_ge(act_out, acts.n)
            keep_order(V.tensor_scalar(f_z[0:8, :], f_z[0:8, :], 0.0, None, ALU.min))
            settle()
            keep_order(V.tensor_tensor(f_a[0:8, :], f_a[0:8, :], f_z[0:8, :], ALU.subtract))
            settle()
            keep_order(V.tensor_tensor_scan(f_z[0:8, :], one_col[0:8].to_broadcast([8, S]), f_a[0:8, :], 0.0,
                                            ALU.mult, ALU.add))
            settle()
            keep_order(V.tensor_scalar(neg_c[0:8, :], f_z[0:8, :], 1.0, None, ALU.mult))
            settle()
            V.tensor_tensor(neg_c[32:40, :], f_z[0:8, :], neg_c[0:8, :].bitcast(F32), ALU.subtract).then_inc(c_ready, 1)
            head_keys()
            finish_rstd(rstd[:, 1, 0:NMEM], rstd_col[:, 4:6])
            head_values()

            def out_to(first_tile):
                def fn(g, b):
                    V.tensor_copy(mix_o[:, first_tile + g, :], b[:]).then_inc(o_taken, 1)
                return fn

            def normed(n):
                name, row, i = ("fox_out_g", rstd_fox, n) if n < 4 else ("sb_out_g", rstd[:, 1, :], n - 4)
                V.scalar_tensor_tensor(mix_o[:, n, :], mix_o[:, n, :], gain(name, i), row,
                                       ALU.mult, ALU.mult).then_inc(t_made, 1)
                made.n += 1

            attention("fox", UNITS, causal, out_to(0),
                      lambda s: mem_keys((s - 7) // 4) if s >= 7 and s % 4 == 3 else None)
            sum_squares(sq_fox, 4)
            head_queries()
            head_keys()
            finish_rstd(rstd_fox)
            head_values()
            keep_order(V.memset(stick[:, S:S + 1], 1.0))
            settle()

            def beside_sb(s):
                if s < 4:
                    normed(s)
                elif 6 <= s < 10:
                    n = s - 6
                    low_half(h_lo[:, n, :], h_hi[:, n, :], mix_o[:, n, :], None, h_ready)
                if s in (7, 11, 15):
                    mem_values_of((s - 7) // 4)
                elif s - 1 in BACK_STEPS:
                    back_tile(BACK_STEPS.index(s - 1) % KT)

            attention("sb", UNITS, strict, out_to(4), beside_sb)

            def low_of_mix(n):
                low_half(h_lo[:, n, :], h_hi[:, n, :], mix_o[:, n, :], None, h_ready)

            sum_squares(sq_sb, 4)
            for n in range(2, 6):
                back_tile(n)
            finish_rstd(rstd[:, 1, :])
            normed(4)
            normed(5)
            back_tile(6)
            back_tile(7)
            for n in (6, 7):
                normed(n)
                low_of_mix(n - 2)
            mem_values_of(3)
            lo_g(3, 0, mix_o[:, 6, :])
            lo_g(3, 1, mix_o[:, 7, :])
            back()
            back("xattn_norm_g")
            sum_squares(sq, KT)
            finish_rstd(rstd[:, 0, :])
            for n in range(KT):
                take(scaled(mem_q[:, n, :], rstd[:, 0, :], 256 ** -0.5))

            def mem_group(g, b):
                lows_done()
                V.tensor_copy(t_buf[:, :, 256 * (g % 2):256 * (g % 2) + 256],
                              b[:].rearrange("p (j n) -> p j n", j=2)).then_inc(o_taken, 1)
                if g % 2:
                    for j in range(2):
                        lo_g(g // 2, j, t_buf[:, j, :])

            attention("mem", MEM_UNITS, None, mem_group,
                      lambda s: [back_tile(2 * (s - 9) % 8 + j) for j in range(2)] if 9 <= s < 20 else None)
            for n in (6, 7):
                back_tile(n)
            back("ffn_norm_g")
            V.memset(conv_u[:, :, 0:2], 0.0)
            V.tensor_tensor(mix0_gain, vec[:, COLUMN["final_norm_g"]:COLUMN["final_norm_g"] + KT],
                            vec[:, COLUMN["mix0"]:COLUMN["mix0"] + KT], ALU.mult)
            sum_squares(sq, KT)
            finish_rstd(rstd[:, 0, :])

            def take_up():
                for j in range(4):
                    take(lambda b: V.tensor_tensor(conv_u[:, j, 2:], b[:], rstd[:, 0, :], ALU.mult))

            def gated(granule, g_reg=0, stride=0, between=lambda: None):
                def w_col(name, j):
                    return gain(name, g_reg * stride + 2 * granule + (j % 2) + 22 * (j // 2))
                for j in range(4):
                    acts.n += 1
                    dve.wait_ge(act_out, acts.at(acts.n))
                    keep_order(V.scalar_tensor_tensor(conv_y[:, j, :], conv_u[:, j, 1:S + 1], w_col("conv_w1", j),
                                                      conv_y[:, j, :], ALU.mult, ALU.add))
                    if j % 2:
                        between()
                for j in range(4):
                    dve.wait_ge(own, mine.at(mine.n - 3 + j))
                    V.scalar_tensor_tensor(conv_y[:, j, :], conv_u[:, j, 0:S], w_col("conv_w0", j),
                                           conv_y[:, j, :], ALU.mult, ALU.add).then_inc(t_made, 1)
                    made.n += 1
                    if j % 2:
                        between()
                dve.wait_ge(t_made, made.at(made.n))
                lows_done()
                for j in range(2):
                    acts.n += 1
                    dve.wait_ge(act_out, acts.at(acts.n))
                    V.tensor_tensor(t_buf[:, j, :], conv_s[:, j, :], conv_y[:, 2 + j, :], ALU.mult).then_inc(t_made, 1)
                    made.n += 1
                    between()
                dve.wait_ge(t_made, made.at(made.n))
                for j in range(2):
                    lo_g(granule, j, t_buf[:, j, :])
                    between()

            def gated_and_back(granule, g_reg=0, stride=0):
                n = iter(range(KT))
                gated(granule, g_reg, stride, lambda: back_tile(next(n)))

            take_up()
            gated(0)
            take_up()
            with loop(dve, 4, [(tile, 24), (hi_n, 4), (g_n, 4), (mine, 8), (acts, 12), (made, 12)]) as i:
                for g in range(2):
                    gated_and_back(1 + g, i, 4)
                    take_up()
            gated_and_back(9)
            take_up()
            gated_and_back(10)
            back("final, mix0")
            sum_squares(sq, KT)
            sum_squares(sq_normed, KT)
            finish_rstd(rstd[:, 0, :], rstd_col[:, 0:4])
            dve.wait_ge(stat_full, stats.n + 1)
            pairs = ((rstd[:, 1, :], rstd[:, 0, :], s_bank[0][:]),
                     (rstd_col[:, 4:8], rstd_col[:, 0:4], col_bank[:, TT:2 * TT]))
            for both, a, m in pairs:
                keep_order(V.tensor_tensor(both, a, m, ALU.mult))
            settle()
            for both, a, m in pairs:
                ins = V.tensor_tensor(both, both, a, ALU.mult)
            ins.then_inc(t_made, 1)
            made.n += 1
            finish_rstd(rstd[:, 1, :], rstd_col[:, 4:8])
            for both, a, m in pairs:
                keep_order(V.tensor_tensor(both, both, a, ALU.mult))
            settle()

            def gate_values(c, reg=0, stride=0):
                for j in range(2):
                    def two_tokens(b):
                        for half in range(2):
                            t = 2 * j + half
                            last = V.tensor_scalar(gm_v[:, t, bass.ds(reg * stride + COLS * c, COLS)],
                                                   b[:, COLS * half:COLS * half + COLS], rstd_col[:, 4 + t:5 + t],
                                                   None, ALU.mult)
                        return last
                    take(two_tokens)

            with loop(dve, 3, [(tile, 4)]) as i:
                gate_values(0, i, 512)
                gate_values(1, i, 512)
            for half in range(2):
                take(lambda b: V.tensor_copy(ws_t[:, 4 * half:4 * half + 4, :], b[:].rearrange("p (g n) -> p g n", n=P)))
            dve.wait_ge(tile_taken, tile.n)
            V.memset(ws_t[64:128, :, 0:64], 0.0).then_inc(gm_ready, 1)
            gate_values(6)
            gate_values(7)
            for half in range(2):
                take(lambda b: V.tensor_copy(ws_sum[:, 4 * half:4 * half + 4, :], b[:].rearrange("p (g n) -> p g n", n=P)))
            acts.n += 16
            dve.wait_ge(act_out, acts.n)
            for t in range(TT):
                for c in range(4):
                    keep_order(V.bn_stats(ln_part[:, c, :], gm_v[:, t, 512 * c:512 * c + 512]))
                settle()
                keep_order(V.bn_aggr(ln_mv[:, t, :], ln_part[:]))
                settle()
            V.tensor_copy(ln_std, ln_mv[:, :, 1]).then_inc(t_made, 1)
            made.n += 1
            for n in range(0, 2):
                take(scaled(gm_u[:, n, :], rstd[:, 1, :]))
            acts.n += 1
            dve.wait_ge(act_out, acts.n)
            keep_order(V.reciprocal(ln_std, ln_std))
            settle()
            for t in range(TT):
                ins = V.tensor_scalar(gm_v[:, t, :], gm_v[:, t, :], ln_mv[:, t, 0:1], ln_std[:, t:t + 1],
                                      ALU.subtract, ALU.mult)
                if t < TT - 1:
                    take(scaled(gm_u[:, 2 + t, :], rstd[:, 1, :]))
            ins.then_inc(gm_ready, 1)
            for n in range(5, 14):
                take(scaled(gm_u[:, n, :], rstd[:, 1, :]))
                if n < 5 + KT:
                    V.scalar_tensor_tensor(x[:, n - 5, :], x[:, n - 5, :], gain("final_norm_g", n - 5),
                                           rstd[:, 0, :], ALU.mult, ALU.mult)

            def gated(g):
                for j in range(2):
                    c = 2 * g + j
                    keep_order(V.scalar_tensor_tensor(biases[:, j, :], ws_sum[:, g, :], gain("a_ln_v_b_2", c),
                                                      bs_all[:, g, :], ALU.mult, ALU.add))
                settle()
                for j in range(2):
                    c = 2 * g + j
                    take(lambda b: V.scalar_tensor_tensor(
                        r_buf[:, j, :].rearrange("p (t n) -> p t n", n=P), b[:].rearrange("p (t n) -> p t n", n=P),
                        gain("a_ln_v_g_2", c), biases[:, j:j + 1, :].to_broadcast([P, TT, P]), ALU.mult, ALU.add))
                acts.n += 2
                dve.wait_ge(act_out, acts.n)
                lows_done()
                for j in range(2):
                    dve.wait_ge(tile_taken, tile.n - 1 + j)
                    V.tensor_tensor(t_buf[:, j, :], r_buf[:, j, :], gm_u[:, 2 * g + j, :], ALU.mult).then_inc(t_made, 1)
                    made.n += 1
                dve.wait_ge(t_made, made.n)
                for j in range(2):
                    lo_g(g, j, t_buf[:, j, :])

            gated(0)
            for n in (14, 15):
                take(scaled(gm_u[:, n, :], rstd[:, 1, :]))
            for g in range(1, 8):
                gated(g)
                back()
            back("mlp0")

            def mlp(following):
                sum_squares(sq, KT)
                finish_rstd(rstd[:, 0, :])

                def up(granule):
                    for j in range(2):
                        take(lambda b: V.scalar_tensor_tensor(r_buf[:, j, :], b[:], 0.0, rstd[:, 0, :],
                                                              ALU.max, ALU.mult))
                    for j in range(2):
                        lo_g(granule, j, t_buf[:, j, :])

                up(0)
                if following == "mix1":
                    V.memset(mla_qr[64:128, :, :], 0.0)
                up(1)
                with loop(dve, 7, [(tile, 20), (hi_n, 4), (g_n, 4)]):
                    for g in range(2):
                        back()
                        up(g)
                back()
                if following:
                    back(following)
                    return
                for n in range(KT):
                    back_tile(n)
                    if n >= 2:
                        add_squares(n - 1)
                add_squares(KT - 1)

            def add_squares(n):
                dve.wait_ge(sq_done, sq_n.n + n + 1)
                settle()
                ins = V.tensor_tensor(sq[:, 0, :], sq[:, 0, :], sq[:, n, :], ALU.add)
                if n < KT - 1:
                    keep_order(ins)
                else:
                    ins.then_inc(acc_ready, 1)

            mlp("mix1")
            sum_squares(sq, KT)
            for n in range(4):
                low_half(g_lo[:, n, :], g_hi[:, n, :], x[:, n, :], gain("kv_src_norm_g_2", n), h_ready)
            finish_rstd(rstd[:, 0, :])
            for n in range(3):
                take(scaled(lat_q[:, n, :], rstd[:, 0, :]))
            for n in range(4, KT):
                lo_h(n, "kv_src_norm_g_2")
            for n in range(3):
                low_half(h_lo[:, n, :], h_hi[:, n, :], lat_q[:, n, :], gain("b_q_norm_g_2", n), h_ready)
            dve.wait_ge(pos_loaded, 32)
            keep_order(V.tensor_copy(ang, pos_i.bitcast(I32)))
            settle()
            keep_order(V.tensor_scalar(ang, ang, invf, None, ALU.mult))
            settle()
            keep_order(V.tensor_scalar(turns, ang, 1.0 / (2 * np.pi), 12582912.0, ALU.mult, ALU.add))
            settle()
            keep_order(V.tensor_scalar(turns, turns, 12582912.0, None, ALU.subtract))
            settle()
            c1 = 6.28125
            c2 = 0.0019350051879882812
            c3 = 2 * np.pi - c1 - c2
            for c in (c1, c2, c3):
                keep_order(V.scalar_tensor_tensor(ang, turns, -c, ang, ALU.mult, ALU.add))
                settle()
            keep_order(V.tensor_scalar(ang, ang, phase, None, ALU.add))
            settle()
            keep_order(V.tensor_scalar(turns, ang, float(np.pi), -2 * np.pi, ALU.is_gt, ALU.mult))
            settle()
            keep_order(V.tensor_tensor(ang, ang, turns, ALU.add))
            settle()
            V.tensor_scalar(ang, ang, 3.1415925, -3.1415925, ALU.min, ALU.max).then_inc(t_made, 1)
            made.n += 1
            for n in range(2):
                take(scaled(lat_kv[:, n, :], rstd[:, 0, :]))
            sum_squares(lat_sq[:, 0:3, :], 3)
            acts.n += 1
            dve.wait_ge(act_out, acts.n)
            keep_order(V.memset(rope_k[:], 0.0))
            settle()

            def turned(b):
                V.tensor_tensor(rope_a[0:64, :], b[0:64, :], rope_t[0:64, :], ALU.mult)
                return V.tensor_tensor(rope_b[0:64, :], b[64:128, :], rope_t[64:128, :], ALU.mult)

            take(lambda b: turned(b))
            dve.wait_ge(tile_taken, tile.n)
            keep_order(V.tensor_tensor(rope_a[0:64, :], rope_a[0:64, :], rope_b[0:64, :], ALU.add))
            settle()
            keep_order(V.tensor_tensor(rope_k[0:64, :], rope_a[0:64, :], rstd[0:64, 0, :], ALU.mult))
            finish_rstd(rstd[:, 1, :])
            scale = (NOPE + ROPE) ** -0.5
            keep_order(V.scalar_tensor_tensor(rope_t[:], rope_t[:], scale, rstd[:, 1, :], ALU.mult, ALU.mult))
            for h in range(MLA_HEADS):
                take(scaled(mla_q[:, h, :], rstd[:, 1, :], scale))
                settle()
                take(lambda b: turned(b))
                dve.wait_ge(tile_taken, tile.n)
                keep_order(V.tensor_tensor(mla_qr[0:64, h, :], rope_a[0:64, :], rope_b[0:64, :], ALU.add))
                if h == 1:
                    sum_squares(lat_sq[:, 3:5, :], 2)
                    for n in range(2):
                        low_half(h_lo[:, 3 + n, :], h_hi[:, 3 + n, :], lat_kv[:, n, :], gain("kv_a_norm_g_2", n),
                                 h_ready)
                if h == 5:
                    finish_rstd(rstd_kv, rstd_col[:, 8:12])
            for c in range(2):
                for h in range(4):
                    take(scaled(mla_k[:, 4 * c + h, :], rstd_kv))
                for t in range(TT):
                    take(lambda b: V.tensor_scalar(mla_v[:, t, 512 * c:512 * c + 512], b[:],
                                                   rstd_col[:, 8 + t:9 + t], None, ALU.mult))

            def mla_group(g, b):
                lows_done()
                V.tensor_copy(t_buf[:, g % 2, :], b[:]).then_inc(o_taken, 1)
                if g % 2:
                    for j in range(2):
                        lo_g(g // 2, j, t_buf[:, j, :])

            attention("mla", UNITS, chunked, mla_group,
                      lambda s: back_tile((s - 13) % 8) if 13 <= s else None)
            back_tile(7)
            back("mlp1")
            mlp(None)

            stats.n += 1
            dve.wait_ge(std_done, stats.n)
            V.reciprocal(rstd_col[:, 0:4], rstd_col[:, 0:4]).then_inc(t_made, 1)
            made.n += 1
            dve.wait_ge(t_made, made.n)
            for q in range(0, len(OUT_PIECES), 2):
                half, t = OUT_PIECES[q]
                dve.wait_ge(out_full, q + 1)
                V.tensor_scalar(out_stage[:, t, 512 * half:512 * half + 512], out_banks(tile.n)[q][:],
                                rstd_col[:, t:t + 1], None, ALU.mult).then_inc(out_vector, 1)

        @block.scalar
        def _(act):
            A = nc.scalar.activation
            tile, hi_n, made, stats, acts, unit = (Count() for _ in range(6))

            act.dma_start(vec_stage, w["vectors"]).then_inc(vec_loaded, 16)
            act.dma_start(b_forget[0:8], w["b_forget"].rearrange("(p a) -> p a", a=1)).then_inc(f_loaded, 16)
            act.dma_start(invf, freq[:] if not hasattr(freq, "ap") else freq.ap()).then_inc(pos_loaded, 16)
            act.wait_ge(consts, CONSTANTS)

            def taken(n=1):
                tile.n += n
                act.wait_ge(tile_taken, tile.at(tile.n))

            def squares(s, n, src):
                A(s[:, n, :], src, ACT.Square).then_inc(sq_done, 1)

            def high_half(dst, src, scale=1.0):
                A(dst, src, ACT.Copy, scale=scale).then_inc(hi_done, 1)
                hi_n.n += 1

            def prep(n, name, s=None):
                if name == "final, mix0":
                    high_half(h_hi[:, n, :], x[:, n, :], mix0_gain[:, n:n + 1])
                elif name:
                    high_half(h_hi[:, n, :], x[:, n, :], gain(name, n))
                squares(sq if s is None else s, n, x[:, n, :])
                if not name:
                    A(y_final[:, n, :], x[:, n, :], ACT.Copy, scale=gain("final_norm_g_2", n)).then_inc(y_ready, 1)

            def root(row, col, row_src, col_src, width):
                stats.n += 1
                act.wait_ge(stat_full, stats.n)
                if row is not None:
                    ins = A(row, row_src, ACT.Sqrt, scale=1.0 / width, bias=eps_t)
                if col is not None:
                    ins = A(col, col_src, ACT.Sqrt, scale=1.0 / width, bias=eps_t)
                ins.then_inc(std_done, 1)

            def back(last=False, name=None):
                if not last:
                    tile.n += KT
                    return
                for n in range(KT):
                    taken()
                    prep(n, name)

            def hi_g(granule, from_t=True):
                for j in range(2):
                    if from_t:
                        made.n += 1
                        act.wait_ge(t_made, made.at(made.n))
                    act.sem_inc(act_gate, 1)
                    high_half(g_hi[:, 2 * (granule % 2) + j, :], t_buf[:, j, :])

            def attention(kind, units, n_after=lambda s: None, n_group=lambda g: None):
                n, per = len(units), GROUP[kind]
                first = unit.n
                for s in range(n + 4):
                    if 0 <= s - 2 < n:
                        u = first + s - 2
                        h, i = units[s - 2]
                        nk = keys(kind, i)
                        act.wait_ge(pt_full, u + 1)
                        if u >= 2:
                            act.wait_ge(pv_done, u - 1)
                        A(prob_t[:, u % 2, 0:nk], pt_bank[:, 0:nk], ACT.Copy).then_inc(pt_taken, 1)
                    if s < n:
                        u = first + s
                        h, i = units[s]
                        nk = keys(kind, i)
                        act.wait_ge(s_masked, u + 1)
                        if u >= 2:
                            act.wait_ge(pt_full, u - 1)
                        src, dst = s_bank[u % 2][:, 0:nk], prob[:, u % 2, 0:nk]
                        if kind == "sb":
                            A(dst, src, ACT.Sigmoid)
                            A(keep[:, u % 2, 0:nk], src, ACT.Sigmoid, scale=-1.0).then_inc(s_taken, 1)
                        else:
                            A(dst, src, ACT.Exp, bias=neg_max[:, u % 2:u % 2 + 1],
                              accum_out=row_sum[:, u % 2:u % 2 + 1]).then_inc(s_taken, 1)
                    if 0 <= s - 3 < n and (s - 3) % per == per - 1:
                        n_group((s - 3) // per)
                    n_after(s)
                unit.n += n

            m_hi = g_hi[:].rearrange("p a b -> p (a b)").rearrange("p (k n) -> p k n", n=NMEM)
            act.wait_ge(own, 1)
            for n in range(KT):
                taken()
                prep(n, "attn_norm_g", sq_x)
            root(rstd[:, 0, :], rstd_col[:, 0:4], stat_bank[:], col_bank[:, 0:4], D)
            tile.n += 4
            for n in range(KT):
                taken()
                high_half(m_hi[:, n, :], mem_t[:, n, :], gain("mem_norm_g", n))
                squares(sq_mem, n, mem_t[:, n, :])
            tile.n += 1
            made.n += 1
            act.wait_ge(t_made, made.n)
            A(f_a[0:8, :], f_z[0:8, :], ACT.Abs).then_inc(act_own, 1)
            act.wait_ge(act_own, 1)
            A(f_a[0:8, :], f_a[0:8, :], ACT.Exp, scale=-1.0).then_inc(act_own, 1)
            act.wait_ge(act_own, 2)
            A(f_a[0:8, :], f_a[0:8, :], ACT.Ln, bias=one_col[0:8]).then_inc(act_out, 1)
            acts.n += 1
            tile.n += 4 + 4
            root(rstd[:, 1, 0:NMEM], rstd_col[:, 4:6], stat_bank[:, 0:NMEM], col_bank[:, 0:2], D)

            def squares_of_group(s, first_tile):
                def fn(g):
                    act.wait_ge(o_taken, first_tile + g + 1)
                    if first_tile:
                        act.wait_ge(h_ready, 2 * KT + g + 1)
                    squares(s, g, mix_o[:, first_tile + g, :])
                return fn

            def fox_halves(s):
                if 4 <= s < 8:
                    made.n += 1
                    act.wait_ge(t_made, made.n)
                    high_half(h_hi[:, s - 4, :], mix_o[:, s - 4, :])

            attention("fox", UNITS, n_group=squares_of_group(sq_fox, 0))
            tile.n += 8
            root(rstd_fox, None, stat_bank[:], None, 512)
            tile.n += 12
            act.wait_ge(tile_taken, tile.n)
            attention("sb", UNITS, fox_halves, squares_of_group(sq_sb, 4))
            tile.n += 1 + 2 * KT + 3
            root(rstd[:, 1, :], None, stat_bank[:], None, 512)
            for n in range(4, 8):
                made.n += 1
                act.wait_ge(t_made, made.n)
                if n == 6:
                    act.wait_ge(tile_taken, tile.n)
                high_half(h_hi[:, n, :] if n < 6 else g_hi[:, n - 4, :], mix_o[:, n, :])
            tile.n += KT
            back(True, "xattn_norm_g")
            root(rstd[:, 0, :], None, stat_bank[:], None, D)
            tile.n += 8
            start_tile, start_group = tile.n, 8

            def mem_split(g):
                if g % 2:
                    act.wait_ge(o_taken, start_group + g + 1)
                    if g // 2 >= 2:
                        act.wait_ge(tile_full, start_tile + 8 * (g // 2 - 1))
                    hi_g(g // 2, from_t=False)
            attention("mem", MEM_UNITS, n_group=mem_split)
            tile.n += 24
            back(True, "ffn_norm_g")
            root(rstd[:, 0, :], None, stat_bank[:], None, D)

            def up(granule, g_reg=0, stride=0):
                for j in range(4):
                    taken()
                    act.sem_inc(act_gate, 1)
                    c = g_reg * stride + 2 * granule + (j % 2) + 22 * (j // 2)
                    A(conv_y[:, j, :], conv_u[:, j, 2:], ACT.Identity, scale=gain("conv_w2", c),
                      bias=gain("conv_b", c)).then_inc(act_out, 1)
                    acts.n += 1
                made.n += 4
                for j in range(2):
                    act.wait_ge(t_made, made.at(made.n - 3 + j))
                    A(conv_s[:, j, :], conv_y[:, j, :], ACT.Silu).then_inc(act_out, 1)
                    acts.n += 1
                hi_g(granule)

            up(0)
            up(1)
            with loop(act, 4, [(tile, 24), (hi_n, 4), (acts, 12), (made, 12)]) as i:
                for g in range(2):
                    back()
                    up(2 + g, i, 4)
            back()
            up(10)
            act.dma_start(ws_stage, w["a_w_s_2"].rearrange("g i j -> i g j")).then_inc(gm_loaded, 16)
            act.dma_start(bs_all, w["a_b_s_2"].partition_broadcast(P)).then_inc(gm_loaded, 16)
            back()
            back(True, "final, mix0")
            for n in range(KT):
                A(sq_normed[:, n, :], x[:, n, :], ACT.Square, scale=gain("final_norm_g", n)).then_inc(sq_done, 1)
            root(rstd[:, 0, :], rstd_col[:, 0:4], stat_bank[:], col_bank[:, 0:4], D)
            made.n += 1
            act.wait_ge(t_made, made.n)
            root(rstd[:, 1, :], rstd_col[:, 4:8], rstd[:, 1, :], rstd_col[:, 4:8], D)
            def gelu_values(at):
                for j in range(2):
                    taken()
                    act.sem_inc(act_gate, 1)
                    v = gm_v[:, 2 * j:2 * j + 2, bass.ds(at, COLS)]
                    A(v, v, ACT.Gelu).then_inc(act_out, 1)
                    acts.n += 1

            def gelu_u(n):
                A(gm_u[:, n, :], gm_u[:, n, :], ACT.Gelu).then_inc(act_out, 1)
                acts.n += 1

            with loop(act, 3, [(tile, 4), (acts, 4)]) as i:
                for c in range(2):
                    gelu_values(i * 512 + COLS * c)
            tile.n += 2
            gelu_values(COLS * 6)
            gelu_values(COLS * 7)
            tile.n += 2
            taken(2)
            made.n += 1
            act.wait_ge(t_made, made.n)
            A(ln_std, ln_std, ACT.Sqrt, bias=eps_t).then_inc(act_out, 1)
            acts.n += 1
            for n in range(14):
                if n >= 2:
                    taken()
                gelu_u(n)
            tile.n += 2
            hi_g(0)
            for n in (14, 15):
                taken()
                gelu_u(n)
            for g in range(1, 8):
                tile.n += 2
                hi_g(g)
                back()
            back(True, "mlp0")

            def mlp(following):
                root(rstd[:, 0, :], None, stat_bank[:], None, D)

                def up(granule):
                    for j in range(2):
                        taken()
                        act.sem_inc(act_gate, 1)
                        A(t_buf[:, j, :], r_buf[:, j, :], ACT.Square)
                        A(g_hi[:, 2 * (granule % 2) + j, :], r_buf[:, j, :], ACT.Square).then_inc(hi_done, 1)
                        hi_n.n += 1

                up(0)
                up(1)
                with loop(act, 7, [(tile, 20), (hi_n, 4)]):
                    for g in range(2):
                        back()
                        up(g)
                back()
                back(True, following)

            mlp("mix1")
            act.dma_start(pos_i.bitcast(I32), w["positions_2"].partition_broadcast(P)).then_inc(pos_loaded, 16)
            for n in range(4):
                high_half(g_hi[:, n, :], x[:, n, :], gain("kv_src_norm_g_2", n))
            root(rstd[:, 0, :], None, stat_bank[:], None, D)
            taken(3)
            for n in range(4, KT):
                high_half(h_hi[:, n, :], x[:, n, :], gain("kv_src_norm_g_2", n))
            for n in range(3):
                high_half(h_hi[:, n, :], lat_q[:, n, :], gain("b_q_norm_g_2", n))
            for n in range(3):
                squares(lat_sq, n, lat_q[:, n, :])
            made.n += 1
            act.wait_ge(t_made, made.n)
            A(rope_t[:], ang, ACT.Sin).then_inc(act_out, 1)
            acts.n += 1
            for n in range(2):
                taken()
                squares(lat_sq, 3 + n, lat_kv[:, n, :])
            taken()
            for n in range(2):
                high_half(h_hi[:, 3 + n, :], lat_kv[:, n, :], gain("kv_a_norm_g_2", n))
            root(rstd[:, 1, :], None, stat_bank[:], None, Q_LORA)
            root(rstd_kv, rstd_col[:, 8:12], stat_bank[:], col_bank[:, 0:4], KV_LORA)
            tile.n += 16 + 16
            start_tile_2, start_group_2 = tile.n, 16

            def mla_split(g):
                if g % 2:
                    act.wait_ge(o_taken, start_group_2 + g + 1)
                    if g // 2 >= 2:
                        act.wait_ge(tile_full, start_tile_2 + 8 * (g // 2 - 1))
                    hi_g(g // 2, from_t=False)
            attention("mla", UNITS, n_group=mla_split)
            tile.n += 24
            back(True, "mlp1")
            mlp(None)
            root(None, rstd_col[:, 0:4], None, col_bank[:, 0:4], D)
            made.n += 1
            act.wait_ge(t_made, made.n)
            for q in range(1, len(OUT_PIECES), 2):
                half, t = OUT_PIECES[q]
                act.wait_ge(out_full, q + 1)
                A(out_stage[:, t, 512 * half:512 * half + 512], out_banks(tile.n)[q][:], ACT.Copy,
                  scale=rstd_col[:, t:t + 1]).then_inc(out_scalar, 1)


def kernel(**inputs):
    import concourse.bacc as bacc
    from concourse.bass_utils import run_bass_kernel_spmd

    nc = bacc.Bacc("TRN2", target_bir_lowering=False, num_devices=1)
    a = {n: np.asarray(v) for n, v in inputs.items()}
    arrays = {}

    def give(name, v):
        arrays[name] = np.ascontiguousarray(v)

    for name in ("x", "mem", "w_in", "b_forget", "w_out", "w_mq", "w_mkv", "w_mo", "w_up", "w_down", "positions_2",
                 "a_w_in_2", "a_b_s_2", "a_w_s_2", "a_w_out_2", "b_w_q_a_2", "b_w_q_b_2", "b_w_o_2"):
        give(name, a[name][0])
    for name in ("kv_w_a_2", "kv_w_b_2"):
        give(name, a[name])
    rows = dict(a)
    for i in range(3):
        rows[f"conv_w{i}"] = a["conv_w"][0, i]
    for i in range(2):
        rows[f"mix{i}"], rows[f"mlp{i}"] = a["norm_mix_g_2"][i], a["norm_mlp_g_2"][i]
    vectors = np.zeros((P, len(VECTORS), P), np.float32)
    for g, group in enumerate(VECTORS):
        r = 0
        for name, n in group:
            vectors[r:r + n, g, :] = rows[name].reshape(n, P)
            r += n
    give("vectors", vectors)
    for i in range(2):
        give(f"w1_{i}", a["mlp_w1_2"][i])
        give(f"w2_{i}", a["mlp_w2_2"][i])
    w = {n: nc.dram_tensor(n, v.shape, mybir.dt.from_np(v.dtype), kind="ExternalInput").ap()
         for n, v in arrays.items()}
    out = nc.dram_tensor("out", (1, S, D), F32, kind="ExternalOutput").ap()
    build(nc, w, out[0])
    r = run_bass_kernel_spmd(nc, [arrays], core_ids=[0])
    return r.results[0]["out"]
```
